# Optimizing a Trainium2 kernel written in Bass

```python
import math
import jax, jax.numpy as jnp
from jax import lax
import numpy as np

D_MODEL = 1024
BATCH = 1
SEQ = 1024
DEPTH = 1

D_MIX = D_MODEL
D_POOL = D_MIX // 2
D_SSM = D_MIX - D_POOL
POOL_WINDOWS = (2, 4, 8, 16)
N_POOL_GROUPS = len(POOL_WINDOWS)
POOL_GROUP = D_POOL // N_POOL_GROUPS
SSM_GROUP = 16
N_SSM_GROUPS = D_SSM // SSM_GROUP
SSM_STATE = 64
D_FF = -(-8 * D_MODEL // (3 * 256)) * 256
RMS_EPS = 1e-6
DT_MIN = 1e-3
DT_MAX = 1e-1


def rmsnorm(x, g):
    xf = x.astype(jnp.float32)
    y = xf * lax.rsqrt(jnp.mean(xf * xf, axis=-1, keepdims=True) + RMS_EPS)
    return y.astype(x.dtype) * g

def pool_mixer(u, w_pool, scale):
    b, l, _ = u.shape
    ug = u.astype(jnp.float32).reshape(b, l, N_POOL_GROUPS, POOL_GROUP)
    cs = jnp.cumsum(ug, axis=1)
    n_pos = jnp.arange(1, l + 1, dtype=jnp.float32)
    diffs = []
    for gi, w in enumerate(POOL_WINDOWS):
        c = cs[:, :, gi]
        lagged = jnp.pad(c, ((0, 0), (w, 0), (0, 0)))[:, :l]
        mean = (c - lagged) / jnp.minimum(n_pos, float(w))[None, :, None]
        diffs.append(mean - ug[:, :, gi])
    d = jnp.stack(diffs, axis=2)
    y = jnp.einsum('blgc,gcd->blgd', d, w_pool.astype(jnp.float32)).reshape(b, l, D_POOL)
    return (y * scale.astype(jnp.float32)).astype(u.dtype)

def _complex_affine_combine(e1, e2):
    a1r, a1i, b1r, b1i = e1
    a2r, a2i, b2r, b2i = e2
    ar = a2r * a1r - a2i * a1i
    ai = a2r * a1i + a2i * a1r
    br = a2r * b1r - a2i * b1i + b2r
    bi = a2r * b1i + a2i * b1r + b2i
    return ar, ai, br, bi

def ssm_mixer(u, lam_re, lam_im, log_dt, b_re, b_im, c_re, c_im, d_skip, w_glu, b_glu):
    f32 = jnp.float32
    bsz, l, _ = u.shape
    ug = u.astype(f32).reshape(bsz, l, N_SSM_GROUPS, SSM_GROUP)
    lr, li = lam_re.astype(f32), lam_im.astype(f32)
    dt = jnp.exp(log_dt.astype(f32))[:, None]
    mag = jnp.exp(lr * dt)
    abar_r = mag * jnp.cos(li * dt)
    abar_i = mag * jnp.sin(li * dt)
    den = lr * lr + li * li
    nr, ni = abar_r - 1.0, abar_i
    coef_r = (nr * lr + ni * li) / den
    coef_i = (ni * lr - nr * li) / den
    br, bi = b_re.astype(f32), b_im.astype(f32)
    bbar_r = coef_r[..., None] * br - coef_i[..., None] * bi
    bbar_i = coef_r[..., None] * bi + coef_i[..., None] * br
    bu_r = jnp.einsum('blgh,gph->blgp', ug, bbar_r)
    bu_i = jnp.einsum('blgh,gph->blgp', ug, bbar_i)
    a_r = jnp.broadcast_to(abar_r, (1, l, N_SSM_GROUPS, SSM_STATE))
    a_i = jnp.broadcast_to(abar_i, (1, l, N_SSM_GROUPS, SSM_STATE))
    _, _, s_r, s_i = lax.associative_scan(_complex_affine_combine, (a_r, a_i, bu_r, bu_i), axis=1)
    y = (jnp.einsum('blgp,ghp->blgh', s_r, c_re.astype(f32))
         - jnp.einsum('blgp,ghp->blgh', s_i, c_im.astype(f32))
         + d_skip.astype(f32) * ug).reshape(bsz, l, D_SSM)
    y = jax.nn.gelu(y)
    y = y * jax.nn.sigmoid(y @ w_glu.astype(f32) + b_glu.astype(f32))
    return y.astype(u.dtype)

def swiglu(h, w_gate, w_up, w_down):
    return (jax.nn.silu(h @ w_gate) * (h @ w_up)) @ w_down

def first_inputs(seed: int = 0) -> dict:
    key = jax.random.key(seed)
    ks = jax.random.split(key, 24)
    f32 = jnp.float32
    nrm = lambda k, s, sc: jax.random.normal(k, s, f32) * sc
    res_scale = (2 * DEPTH) ** -0.5
    n_idx = jnp.arange(SSM_STATE, dtype=f32)
    lam_re = -0.5 + nrm(ks[5], (DEPTH, N_SSM_GROUPS, SSM_STATE), 0.01)
    lam_im = math.pi * n_idx[None, None, :] + nrm(ks[6], (DEPTH, N_SSM_GROUPS, SSM_STATE), 0.01)
    log_dt = jax.random.uniform(ks[7], (DEPTH, N_SSM_GROUPS), f32, math.log(DT_MIN), math.log(DT_MAX))
    return {
        "x": nrm(ks[0], (BATCH, SEQ, D_MODEL), 1.0),
        "norm_mix": 1.0 + nrm(ks[1], (DEPTH, D_MODEL), 0.02),
        "w_in": nrm(ks[2], (DEPTH, D_MODEL, D_MIX), D_MODEL ** -0.5),
        "w_pool": nrm(ks[3], (DEPTH, N_POOL_GROUPS, POOL_GROUP, POOL_GROUP), POOL_GROUP ** -0.5),
        "pool_scale": 1.0 + nrm(ks[4], (DEPTH, D_POOL), 0.02),
        "lam_re": lam_re,
        "lam_im": lam_im,
        "log_dt": log_dt,
        "b_re": nrm(ks[8], (DEPTH, N_SSM_GROUPS, SSM_STATE, SSM_GROUP), (2 * SSM_GROUP) ** -0.5),
        "b_im": nrm(ks[9], (DEPTH, N_SSM_GROUPS, SSM_STATE, SSM_GROUP), (2 * SSM_GROUP) ** -0.5),
        "c_re": nrm(ks[10], (DEPTH, N_SSM_GROUPS, SSM_GROUP, SSM_STATE), (2 * SSM_STATE) ** -0.5),
        "c_im": nrm(ks[11], (DEPTH, N_SSM_GROUPS, SSM_GROUP, SSM_STATE), (2 * SSM_STATE) ** -0.5),
        "d_skip": nrm(ks[12], (DEPTH, N_SSM_GROUPS, SSM_GROUP), 1.0),
        "w_glu": nrm(ks[13], (DEPTH, D_SSM, D_SSM), D_SSM ** -0.5),
        "b_glu": nrm(ks[14], (DEPTH, D_SSM), 0.01),
        "w_out": nrm(ks[15], (DEPTH, D_MIX, D_MODEL), D_MIX ** -0.5 * res_scale),
        "norm_ffn": 1.0 + nrm(ks[16], (DEPTH, D_MODEL), 0.02),
        "w_gate": nrm(ks[17], (DEPTH, D_MODEL, D_FF), D_MODEL ** -0.5),
        "w_up": nrm(ks[18], (DEPTH, D_MODEL, D_FF), D_MODEL ** -0.5),
        "w_down": nrm(ks[19], (DEPTH, D_FF, D_MODEL), D_FF ** -0.5 * res_scale),
        "norm_final": 1.0 + nrm(ks[20], (D_MODEL,), 0.02),
    }

def first_block(x, norm_mix, w_in, w_pool, pool_scale, lam_re, lam_im, log_dt, b_re, b_im,
              c_re, c_im, d_skip, w_glu, b_glu, w_out, norm_ffn, w_gate, w_up, w_down,
              norm_final):
    h = x
    for i in range(DEPTH):
        u = rmsnorm(h, norm_mix[i]) @ w_in[i]
        u_pool, u_ssm = u[..., :D_POOL], u[..., D_POOL:]
        y_pool = pool_mixer(u_pool, w_pool[i], pool_scale[i])
        y_ssm = ssm_mixer(u_ssm, lam_re[i], lam_im[i], log_dt[i], b_re[i], b_im[i],
                          c_re[i], c_im[i], d_skip[i], w_glu[i], b_glu[i])
        h = h + jnp.concatenate([y_pool, y_ssm], axis=-1) @ w_out[i]
        h = h + swiglu(rmsnorm(h, norm_ffn[i]), w_gate[i], w_up[i], w_down[i])
    return rmsnorm(h, norm_final)


MLA_HEADS = 8
QK_NOPE_DIM = 64
QK_ROPE_DIM = 32
QK_HEAD_DIM = QK_NOPE_DIM + QK_ROPE_DIM
V_HEAD_DIM = 64
Q_LORA_RANK = 384
KV_LORA_RANK = 256
ROPE_THETA = 10000.0
Q_BLOCK = 128
RWKV_HEADS = 8
RWKV_HEAD_DIM = 64
RWKV_DIM = RWKV_HEADS * RWKV_HEAD_DIM
DECAY_LORA = 64
AAA_LORA = 64
GATE_LORA = 128
GN_EPS = RWKV_HEAD_DIM * 1e-5
MLA_COLS = Q_LORA_RANK + KV_LORA_RANK + QK_ROPE_DIM
RWKV_COLS = 3 * RWKV_DIM + DECAY_LORA + AAA_LORA + GATE_LORA
GATE_COLS = 2 * D_MODEL
IN_COLS = MLA_COLS + RWKV_COLS + GATE_COLS
D_FF_2 = 4 * D_MODEL
PLE_DIM = 256


def rmsnorm_2(x, g):
    xf = x.astype(jnp.float32)
    y = xf * lax.rsqrt(jnp.mean(xf * xf, axis=-1, keepdims=True) + RMS_EPS)
    return (y * g.astype(jnp.float32)).astype(x.dtype)

def rope_tables(positions):
    half = QK_ROPE_DIM // 2
    inv_freq = ROPE_THETA ** (-jnp.arange(half, dtype=jnp.float32) / half)
    ang = positions.astype(jnp.float32)[..., None] * inv_freq
    return jnp.cos(ang), jnp.sin(ang)

def apply_rope(x, cos, sin):
    xf = x.astype(jnp.float32)
    x1, x2 = jnp.split(xf, 2, axis=-1)
    out = jnp.concatenate([x1 * cos - x2 * sin, x2 * cos + x1 * sin], axis=-1)
    return out.astype(x.dtype)

def causal_block_attention(q, k, v, scale):
    S = q.shape[1]
    outs = []
    for blk in range(S // Q_BLOCK):
        q0 = blk * Q_BLOCK
        kend = q0 + Q_BLOCK
        qb = q[:, q0:kend]
        s = jnp.einsum('bqhd,bkhd->bhqk', qb, k[:, :kend]).astype(jnp.float32) * scale
        mask = jnp.arange(kend)[None, :] <= (q0 + jnp.arange(Q_BLOCK))[:, None]
        s = jnp.where(mask, s, jnp.float32(-1e30))
        prob = jax.nn.softmax(s, axis=-1).astype(v.dtype)
        outs.append(jnp.einsum('bhqk,bkhd->bqhd', prob, v[:, :kend]))
    return jnp.concatenate(outs, axis=1)

def mla_branch(z, cos, sin, g_q_a, w_uq, g_kv_a, w_ukv, w_o_mla):
    B, S, _ = z.shape
    c_q, c_kv, k_pe = jnp.split(z, [Q_LORA_RANK, Q_LORA_RANK + KV_LORA_RANK], axis=-1)
    q = (rmsnorm_2(c_q, g_q_a) @ w_uq).reshape(B, S, MLA_HEADS, QK_HEAD_DIM)
    q_nope, q_pe = jnp.split(q, [QK_NOPE_DIM], axis=-1)
    q_pe = apply_rope(q_pe, cos[:, :, None, :], sin[:, :, None, :])
    kv = (rmsnorm_2(c_kv, g_kv_a) @ w_ukv).reshape(B, S, MLA_HEADS, QK_NOPE_DIM + V_HEAD_DIM)
    k_nope, v = jnp.split(kv, [QK_NOPE_DIM], axis=-1)
    k_pe = apply_rope(k_pe, cos, sin)
    qh = jnp.concatenate([q_nope, q_pe], axis=-1)
    kh = jnp.concatenate([k_nope, jnp.broadcast_to(k_pe[:, :, None, :], (B, S, MLA_HEADS, QK_ROPE_DIM))], axis=-1)
    o = causal_block_attention(qh, kh, v, QK_HEAD_DIM ** -0.5)
    return o.reshape(B, S, MLA_HEADS * V_HEAD_DIM) @ w_o_mla

def token_shift(z, mu):
    prev = jnp.pad(z, ((0, 0), (1, 0), (0, 0)))[:, :-1]
    return z + (prev - z) * mu

def wkv7_scan(r, decay, k, v, a_vec, b_vec):
    B, S, H, N = r.shape

    def step(state, inp):
        r_t, d_t, k_t, v_t, a_t, b_t = inp
        sa = jnp.einsum('bhvk,bhk->bhv', state, a_t)
        state = (state * d_t[:, :, None, :] + sa[..., None] * b_t[:, :, None, :]
                 + v_t[..., None] * k_t[:, :, None, :])
        return state, jnp.einsum('bhvk,bhk->bhv', state, r_t)

    xs = tuple(jnp.moveaxis(t, 1, 0) for t in (r, decay, k, v, a_vec, b_vec))
    _, ys = lax.scan(step, jnp.zeros((B, H, N, N), jnp.float32), xs)
    return jnp.moveaxis(ys, 0, 1)

def rwkv7_branch(z, mu_rwkv, w0, w2, a0, a2, g2, k_k, k_a, r_k, ln_x_w, ln_x_b, w_o_rwkv):
    B, S, _ = z.shape
    f32 = jnp.float32
    z = token_shift(z, mu_rwkv)
    r, k, v, w_lo, a_lo, g_lo = jnp.split(
        z, [RWKV_DIM, 2 * RWKV_DIM, 3 * RWKV_DIM, 3 * RWKV_DIM + DECAY_LORA,
            3 * RWKV_DIM + DECAY_LORA + AAA_LORA], axis=-1)
    w_log = -jax.nn.softplus(-(w0.astype(f32) + (jnp.tanh(w_lo) @ w2).astype(f32))) - 0.5
    decay = jnp.exp(-jnp.exp(w_log))
    a = jax.nn.sigmoid(a0.astype(f32) + (a_lo @ a2).astype(f32))
    g = jax.nn.sigmoid(g_lo) @ g2
    hs = (B, S, RWKV_HEADS, RWKV_HEAD_DIM)
    r = r.astype(f32).reshape(hs)
    k = k.astype(f32)
    v = v.astype(f32).reshape(hs)
    kk = (k * k_k.astype(f32)).reshape(hs)
    kk = kk / jnp.maximum(jnp.linalg.norm(kk, axis=-1, keepdims=True), 1e-12)
    k = (k * (1.0 + (a - 1.0) * k_a.astype(f32))).reshape(hs)
    a = a.reshape(hs)
    decay = decay.reshape(hs)
    y = wkv7_scan(r, decay, k, v, -kk, kk * a)
    mean = jnp.mean(y, axis=-1, keepdims=True)
    var = jnp.mean(jnp.square(y - mean), axis=-1, keepdims=True)
    y = ((y - mean) * lax.rsqrt(var + GN_EPS)).reshape(B, S, RWKV_DIM)
    y = y * ln_x_w.astype(f32) + ln_x_b.astype(f32)
    bonus = jnp.sum(r * k * r_k.astype(f32), axis=-1, keepdims=True) * v
    y = (y + bonus.reshape(B, S, RWKV_DIM)).astype(z.dtype) * g
    return y @ w_o_rwkv

def second_inputs(seed: int = 0) -> dict:
    key = jax.random.key(seed)
    ks = jax.random.split(key, 40)
    f32 = jnp.float32
    L = DEPTH

    def nrm(k, shape, fan_in):
        return jax.random.normal(k, shape, f32) * (fan_in ** -0.5)

    def gain(k, shape):
        return 1.0 + 0.02 * jax.random.normal(k, shape, f32)

    H, N = RWKV_HEADS, RWKV_HEAD_DIM
    return {
        "x": jax.random.normal(ks[0], (BATCH, SEQ, D_MODEL), f32),
        "p": jax.random.normal(ks[1], (DEPTH, BATCH, SEQ, PLE_DIM), f32),
        "positions": (jax.random.randint(ks[2], (BATCH, 1), 0, 1024, jnp.int32)
                      + jnp.arange(SEQ, dtype=jnp.int32)[None, :]),
        "g_mix": gain(ks[3], (L, D_MODEL)),
        "w_in": nrm(ks[4], (L, D_MODEL, IN_COLS), D_MODEL),
        "g_q_a": gain(ks[5], (L, Q_LORA_RANK)),
        "w_uq": nrm(ks[6], (L, Q_LORA_RANK, MLA_HEADS * QK_HEAD_DIM), Q_LORA_RANK),
        "g_kv_a": gain(ks[7], (L, KV_LORA_RANK)),
        "w_ukv": nrm(ks[8], (L, KV_LORA_RANK, MLA_HEADS * (QK_NOPE_DIM + V_HEAD_DIM)), KV_LORA_RANK),
        "w_o_mla": nrm(ks[9], (L, MLA_HEADS * V_HEAD_DIM, D_MODEL), MLA_HEADS * V_HEAD_DIM),
        "mu_rwkv": jax.random.uniform(ks[10], (L, RWKV_COLS), f32),
        "w0": jax.random.uniform(ks[11], (L, RWKV_DIM), f32, -6.5, -1.5),
        "w2": nrm(ks[12], (L, DECAY_LORA, RWKV_DIM), DECAY_LORA),
        "a0": 0.1 * jax.random.normal(ks[13], (L, RWKV_DIM), f32),
        "a2": nrm(ks[14], (L, AAA_LORA, RWKV_DIM), AAA_LORA),
        "g2": nrm(ks[15], (L, GATE_LORA, RWKV_DIM), GATE_LORA),
        "k_k": 0.85 + 0.02 * jax.random.normal(ks[16], (L, RWKV_DIM), f32),
        "k_a": gain(ks[17], (L, RWKV_DIM)),
        "r_k": 0.1 * jax.random.normal(ks[18], (L, H, N), f32),
        "ln_x_w": gain(ks[19], (L, RWKV_DIM)),
        "ln_x_b": 0.02 * jax.random.normal(ks[20], (L, RWKV_DIM), f32),
        "w_o_rwkv": nrm(ks[21], (L, RWKV_DIM, D_MODEL), RWKV_DIM),
        "w_out": nrm(ks[22], (L, D_MODEL, D_MODEL), D_MODEL),
        "g_ffn": gain(ks[23], (L, D_MODEL)),
        "w_ffn_up": nrm(ks[24], (L, D_MODEL, D_FF_2), D_MODEL),
        "w_ffn_down": nrm(ks[25], (L, D_FF_2, D_MODEL), D_FF_2),
        "g_ple": gain(ks[26], (L, D_MODEL)),
        "w_ple_gate": nrm(ks[27], (L, D_MODEL, D_MODEL), D_MODEL),
        "w_ple_proj": nrm(ks[28], (L, PLE_DIM, D_MODEL), PLE_DIM),
        "g_final": gain(ks[29], (D_MODEL,)),
    }

def second_block(x, p, positions, g_mix, w_in, g_q_a, w_uq, g_kv_a, w_ukv, w_o_mla,
              mu_rwkv, w0, w2, a0, a2, g2, k_k, k_a, r_k, ln_x_w, ln_x_b, w_o_rwkv,
              w_out, g_ffn, w_ffn_up, w_ffn_down, g_ple, w_ple_gate, w_ple_proj, g_final):
    cos, sin = rope_tables(positions)
    for i in range(DEPTH):
        h = rmsnorm_2(x, g_mix[i])
        z = h @ w_in[i]
        z_mla, z_rwkv, z_gate = jnp.split(z, [MLA_COLS, MLA_COLS + RWKV_COLS], axis=-1)
        y_a = mla_branch(z_mla, cos, sin, g_q_a[i], w_uq[i], g_kv_a[i], w_ukv[i], w_o_mla[i])
        y_b = rwkv7_branch(z_rwkv, mu_rwkv[i], w0[i], w2[i], a0[i], a2[i], g2[i], k_k[i], k_a[i],
                           r_k[i], ln_x_w[i], ln_x_b[i], w_o_rwkv[i])
        gate = jax.nn.sigmoid(z_gate)
        gate_a, gate_b = jnp.split(gate, 2, axis=-1)
        x = x + (gate_a * y_a + gate_b * y_b) @ w_out[i]
        h = rmsnorm_2(x, g_ffn[i])
        x = x + jnp.square(jax.nn.relu(h @ w_ffn_up[i])) @ w_ffn_down[i]
        ple_gate = jax.nn.sigmoid(rmsnorm_2(x, g_ple[i]) @ w_ple_gate[i])
        x = x + ple_gate * (p[i] @ w_ple_proj[i])
    return rmsnorm_2(x, g_final)


_first_inputs = second_inputs


def second_inputs(seed=0):
    import zlib

    import numpy as np

    out = dict(_first_inputs(seed))
    spreads = {}
    factors = {'g_mix': 5.058,
     'g_q_a': 49.471,
     'g_kv_a': 56.252,
     'w2': 16.471,
     'a0': 5.452,
     'k_k': 64.0,
     'k_a': 8.0,
     'ln_x_w': 64.0,
     'ln_x_b': 64.0,
     'g_ffn': 27.832,
     'g_ple': 64.0,
     'g_final': 8.488,
     'p': 7.018,
     'w0': 3.919,
     'w_ple_gate': 8.0,
     'w_ple_proj': 7.024}
    for name, (base, spread) in spreads.items():
        noise = np.random.default_rng([zlib.crc32(name.encode()), seed]).standard_normal(out[name].shape)
        drawn = base * np.exp(spread * noise) if base else spread * noise
        out[name] = __import__('jax').numpy.asarray(drawn.astype(out[name].dtype))
    for name, factor in factors.items():
        out[name] = (out[name] * factor).astype(out[name].dtype)
    return out


_narrow_inputs = second_inputs


def second_inputs(seed=0):

    out = dict(_narrow_inputs(seed))
    wider = {'k_k': 12.0, 'ln_x_w': 10.22, 'ln_x_b': 10.24, 'g_ple': 12.0, 'g_final': 3.25}
    for name, times in wider.items():
        mean = out[name].mean()
        out[name] = (mean + times * (out[name] - mean)).astype(out[name].dtype)
    return out


def setup_inputs(seed=0):
    out = dict(first_inputs(seed))
    for name, value in second_inputs(seed + 1).items():
        if name != "x":
            out[name + "_2"] = value
    return out


def reference(
    x, norm_mix, w_in, w_pool, pool_scale, lam_re, lam_im, log_dt, b_re, b_im, c_re, c_im,
    d_skip, w_glu, b_glu, w_out, norm_ffn, w_gate, w_up, w_down, norm_final, p_2, positions_2,
    g_mix_2, w_in_2, g_q_a_2, w_uq_2, g_kv_a_2, w_ukv_2, w_o_mla_2, mu_rwkv_2, w0_2, w2_2, a0_2,
    a2_2, g2_2, k_k_2, k_a_2, r_k_2, ln_x_w_2, ln_x_b_2, w_o_rwkv_2, w_out_2, g_ffn_2,
    w_ffn_up_2, w_ffn_down_2, g_ple_2, w_ple_gate_2, w_ple_proj_2, g_final_2,
):
    x = first_block(
        x, norm_mix, w_in, w_pool, pool_scale, lam_re, lam_im, log_dt, b_re, b_im, c_re, c_im,
        d_skip, w_glu, b_glu, w_out, norm_ffn, w_gate, w_up, w_down, norm_final,
    )
    return second_block(
        x, p_2, positions_2, g_mix_2, w_in_2, g_q_a_2, w_uq_2, g_kv_a_2, w_ukv_2, w_o_mla_2,
        mu_rwkv_2, w0_2, w2_2, a0_2, a2_2, g2_2, k_k_2, k_a_2, r_k_2, ln_x_w_2, ln_x_b_2,
        w_o_rwkv_2, w_out_2, g_ffn_2, w_ffn_up_2, w_ffn_down_2, g_ple_2, w_ple_gate_2,
        w_ple_proj_2, g_final_2,
    )


_drawn_inputs = setup_inputs


def setup_inputs(seed=0):
    import zlib

    import numpy as np

    out = dict(_drawn_inputs(seed))
    spreads = {}
    factors = {'lam_re': 8.0, 'b_glu': 3.994, 'g_ple_2': 4.704}
    for name, (base, spread) in spreads.items():
        noise = np.random.default_rng([zlib.crc32(name.encode()), seed]).standard_normal(out[name].shape)
        drawn = base * np.exp(spread * noise) if base else spread * noise
        out[name] = __import__('jax').numpy.asarray(drawn.astype(out[name].dtype))
    for name, factor in factors.items():
        out[name] = (out[name] * factor).astype(out[name].dtype)
    return out
```

```python
import math
from contextlib import ExitStack

import numpy as np
import concourse.bass as bass
from concourse import mybir

F32 = mybir.dt.float32
F32R = mybir.dt.float32r
I32 = mybir.dt.int32
ALU = mybir.AluOpType
ACT = mybir.ActivationFunctionType
AX = mybir.AxisListType

P = 128
L = 1024
D = 1024
KD = D // P
HALF = 512
DFF = 2816
DFF2 = 4096
EPS = 1e-6
WINDOWS = (2, 4, 8, 16)
SG, SH, SP_ = 32, 16, 64
SJ = 8
SC = L // SJ
GB = 8
NH, QN, QR, VD = 8, 64, 32, 64
QH = QN + QR
QLORA, KVLORA = 384, 256
C = 64
NC = L // C
NPAIR = 4
GN_EPS = 64 * 1e-5
DECAY = math.exp(-0.5)
MLA_COLS = QLORA + KVLORA + QR
RWKV_COLS = 3 * 512 + 64 + 64 + 128
TWO_PI = 2 * math.pi
MAGIC = 1.5 * 2.0 ** 23


class Count:

    def __init__(self, sem):
        self.sem, self.value = sem, 0

    def add(self, n):
        self.value += n
        return (self, self.value)


class Stream:

    def __init__(self, count, chained):
        self.done, self.chained = count, chained
        self.steps, self.seen = [], {}

    def wait(self, *marks):
        for mark in marks:
            if mark is None:
                continue
            if isinstance(mark, list):
                self.wait(*mark)
                continue
            count, value = mark
            if value > self.seen.get(id(count), 0):
                self.seen[id(count)] = value
                self.steps.append(("wait", count.sem, value))

    def do(self, make, *marks, signal=True):
        self.wait(*marks)
        if self.chained and self.done.value:
            self.wait((self.done, self.done.value))
        if not signal:
            self.steps.append(("do", make, None, 0))
            return None
        self.steps.append(("do", make, self.done.sem, 1))
        return self.done.add(1)

    def dma(self, count, out, in_, *marks):
        self.wait(*marks)
        self.steps.append(("do", lambda e: e.dma_start(out, in_), count.sem, 16))
        return count.add(16)

    def play(self, engine):
        for kind, what, *rest in self.steps:
            if kind == "wait":
                engine.wait_ge(what, rest[0])
            else:
                ins = what(engine)
                if rest[0] is not None:
                    ins.then_inc(rest[0], rest[1])


class Ring:

    def __init__(self, tiles, counts=None):
        self.tiles, self.counts = tiles, counts
        self.free = [[] for _ in tiles]
        self.at = -1

    def take(self):
        self.at = (self.at + 1) % len(self.tiles)
        return self.at, self.tiles[self.at], self.free[self.at]

    def release(self, n, *marks):
        self.free[n] = list(marks)


def build(nc, a, out):
    main = ExitStack()
    counts = []

    def count(name):
        c = Count(main.enter_context(nc.semaphore(name)))
        counts.append(c)
        return c

    V = Stream(count("vector_done"), True)
    S = Stream(count("scalar_done"), True)
    G = Stream(count("gpsimd_done"), True)
    T = Stream(count("tensor_done"), False)
    Q = Stream(count("sync_done"), False)
    streams = [V, S, G, T, Q]

    def finish():
        Q.wait(*[(c, c.value) for c in counts if c is not Q.done])
        with nc.Block() as block:
            for stream, on in ((V, block.vector), (S, block.scalar), (G, block.gpsimd), (T, block.tensor),
                               (Q, block.sync)):
                on(stream.play)

    names = [0]

    def sb(ctx, name, shape, dt=F32):
        names[0] += 1
        return ctx.enter_context(nc.sbuf_tensor(f"{name}_{names[0]}", shape, dt))

    def fence():
        for s in streams:
            s.wait(*[(c, c.value) for c in counts if c is not s.done or s.chained])

    banks = Ring([main.enter_context(nc.psum_tensor(f"bank{i}", [P, HALF], F32)) for i in range(8)])

    def dram(name, shape):
        return nc.dram_tensor(name, shape, F32).ap()

    z_dram = dram("z_scratch", [36 * P, L])
    x_dram = dram("x_scratch", [D, L])
    n_dram = dram("n_scratch", [P, C * C])
    r_dram = dram("r_scratch", [P, C * C])
    rw_dram = dram("rwkv_scratch", [512, L])
    g_dram = dram("gate_scratch", [512, L])
    bonus_dram = dram("bonus_scratch", [512, L])
    mla_dram = dram("mla_scratch", [512, L])

    c_const = count("consts_in")
    const = {}

    def load_const(name, ap, shape, dt=F32):
        t = sb(main, name, shape, dt)
        Q.dma(c_const, t[:], ap)
        const[name] = t
        return t

    ident = load_const("ident", a["k_ident"], [P, P])
    headones = load_const("headones", a["k_headones"], [P, P])
    ones = load_const("ones", a["k_ones"], [P, P])
    kvec = load_const("kvec", a["k_vec"], [P, 16])
    channel_vectors = (("norm_mix", D), ("norm_ffn", D), ("pool_scale", 512), ("b_glu", 512),
                       ("norm_final", D), ("g_mix_2", D), ("g_q_a_2", QLORA), ("g_kv_a_2", KVLORA),
                       ("mu_rwkv_2", RWKV_COLS), ("w0_2", 512), ("a0_2", 512), ("k_k_2", 512), ("k_a_2", 512),
                       ("r_k_2", 512), ("ln_x_w_2", 512), ("ln_x_b_2", 512), ("g_ffn_2", D), ("g_ple_2", D),
                       ("g_final_2", D))
    vec_rows = sb(main, "vec_rows", [P, P])
    vec_cols = sb(main, "vec_cols", [P, P])
    vec, row = {}, 0
    for name, n in channel_vectors:
        v = a[name] if len(a[name].shape) == 1 else a[name][0]
        v = v.rearrange("h n -> (h n)") if len(v.shape) == 2 else v
        Q.dma(c_const, vec_rows[row:row + n // P, :], v.rearrange("(k p) -> k p", p=P))
        vec[name] = vec_cols[:, row:row + n // P]
        row += n // P
    n_vec = row
    consts_in = (c_const, c_const.value)
    eps_col, gn_eps_col, sign_pm, sign_mp, minus_one, inv_freq, rope_sign = (
        kvec[:, i:i + 1] for i in range(7))
    for s in (V, S, G, T):
        s.wait(consts_in)

    n, ps, free = banks.take()
    m = T.do(lambda e, ps=ps: e.transpose(ps[:, 0:n_vec], vec_rows[0:n_vec, :], ident[0:n_vec, 0:n_vec]))
    m = V.do(lambda e, ps=ps: e.tensor_copy(vec_cols[:, 0:n_vec], ps[:, 0:n_vec]), m)
    banks.release(n, m)
    for s in (S, G):
        s.wait(m)

    rs = sb(main, "rs", [P, L])
    rs_ready = [None]

    def evac_engine(n):
        return V if n % 2 == 0 else S

    def copy(eng, o, i, *marks):
        if eng is S:
            return S.do(lambda e: e.activation(o, i, ACT.Copy), *marks)
        return eng.do(lambda e: e.tensor_copy(o, i), *marks)

    def tt(eng, o, x, y, op, *marks):
        return eng.do(lambda e: e.tensor_tensor(o, x, y, op), *marks)

    def ts(eng, o, x, s1, s2, op0, op1, *marks):
        if s2 is None:
            return eng.do(lambda e: e.tensor_scalar(o, x, s1, None, op0), *marks)
        return eng.do(lambda e: e.tensor_scalar(o, x, s1, s2, op0, op1), *marks)

    def stt(o, x, s1, y, op0, op1, *marks):
        return V.do(lambda e: e.scalar_tensor_tensor(out=o, in0=x, scalar=s1, in1=y, op0=op0, op1=op1),
                    *marks)

    def act(o, x, f, *marks, **kw):
        return S.do(lambda e: e.activation(o, x, f, **kw), *marks)

    def mm(o, w, x, start, stop, *marks, signal=None):
        return T.do(lambda e: e.matmul(o, w, x, start=start, stop=stop), *marks,
                    signal=stop if signal is None else signal)

    def transpose(o, i, *marks):
        return T.do(lambda e: e.transpose(o, i, ident[0:i.shape[0], 0:i.shape[0]]), *marks)

    class Weights:

        SIZE = 2048

        def __init__(self, ctx, plan, raw=3, parts=2):
            self.RAW, self.PARTS = raw, parts
            self.raw = Ring([sb(ctx, "w_raw", [P, self.SIZE]) for _ in range(self.RAW)],
                            [count(f"w_in_{names[0]}_{i}") for i in range(self.RAW)])
            self.hi = [sb(ctx, "w_hi", [P, self.SIZE], F32R) for _ in range(self.PARTS)]
            self.lo = [sb(ctx, "w_lo", [P, self.SIZE], F32R) for _ in range(self.PARTS)]
            self.used = [[] for _ in range(self.PARTS)]
            self.plan, self.loaded, self.split, self.next = plan, {}, {}, 0
            for i in range(min(self.RAW, len(plan))):
                self.load(i)

        def load(self, i):
            kt, cols, pieces = self.plan[i]
            n, tile, free = self.raw.take()
            view = tile[:, 0:kt * cols].rearrange("p (k c) -> p k c", k=kt)
            for c0, src in pieces:
                self.loaded[i] = (n, Q.dma(self.raw.counts[n], view[:, :, c0:c0 + src.shape[2]], src, free))

        def split_block(self, i):
            kt, cols, _ = self.plan[i]
            n, here = self.loaded.pop(i)
            size = kt * cols
            raw, hi, lo = (t[:, 0:size] for t in (self.raw.tiles[n], self.hi[i % self.PARTS], self.lo[i % self.PARTS]))
            m1 = copy(S, hi, raw, here, self.used[i % self.PARTS])
            m2 = tt(V, lo, raw, hi, ALU.subtract, here, m1, self.used[i % self.PARTS])
            self.raw.release(n, m1, m2)
            view = lambda t: t.rearrange("p (k c) -> p k c", k=kt)
            self.split[i] = (view(hi), view(lo), [m1, m2])

        def take(self):
            i = self.next
            self.next += 1
            if i not in self.split:
                self.split_block(i)
            if self.PARTS > 1 and i + 1 < len(self.plan) and i + 1 not in self.split:
                self.split_block(i + 1)
            for j in range(i + self.PARTS, i + self.PARTS + self.RAW):
                if j < len(self.plan) and j not in self.loaded and j not in self.split:
                    self.load(j)
            return self.split.pop(i)

        def done(self, mark):
            self.used[(self.next - 1) % self.PARTS] = [mark]

    def wblock(w, k0, kt, c0, cols):
        return (kt, cols, [(0, w[k0:k0 + kt * P, c0:c0 + cols].rearrange("(k p) c -> p k c", p=P))])

    def product(ps, pairs, *marks):
        m = None
        for i, (w, x) in enumerate(pairs):
            m = mm(ps, w, x, i == 0, i == len(pairs) - 1, *(marks if i == 0 else ()))
        return m

    def three(w, x, kt, wc, xc):
        out_ = []
        for k in range(kt):
            out_ += [(w[0][:, k, wc], x[0][:, k, xc]), (w[0][:, k, wc], x[1][:, k, xc]),
                     (w[1][:, k, wc], x[0][:, k, xc])]
        return out_

    def linear(weights, x, kt, tiles, evac, ready):
        hi, lo, there = weights.take()
        last = None
        for c0, index in tiles:
            for half in range(2):
                n, ps, free = banks.take()
                last = product(ps[:], three((hi, lo), x, kt, slice(c0, c0 + P),
                                            slice(half * HALF, half * HALF + HALF)),
                               free, there, ready)
                banks.release(n, *evac(index, half, ps, last))
        weights.done(last)

    def hs(half):
        return slice(half * HALF, half * HALF + HALF)

    def split_scaled(hT, g, hi, lo, *marks):
        out_ = []
        for k in range(KD):
            gk = g[:, k:k + 1]
            m = act(hi[:, k, :], hT[:, k, :], ACT.Copy, *marks, scale=gk)
            out_ = [m, stt(lo[:, k, :], hT[:, k, :], gk, hi[:, k, :], ALU.mult, ALU.subtract, m, *marks)]
        return out_

    def inverse_rms(ctx, sq_sum_bank_fn, dst, n, *marks):
        out_ = []
        for half in range(2):
            nb, ps, m = sq_sum_bank_fn(half)
            m1 = act(dst[:, hs(half)], ps[:], ACT.Sqrt, m, *marks, bias=eps_col, scale=1.0 / n)
            banks.release(nb, m1)
            out_.append(V.do(lambda e, h=half: e.reciprocal(dst[:, hs(h)], dst[:, hs(h)]), m1))
        return out_

    def norm(ctx, x, kt, dst, n, *marks):
        sq = [sb(ctx, "sq", [P, L]) for _ in range(2)]
        acc = sb(ctx, "sq_sum", [P, L])
        m = None
        freed = [None, None]
        for k in range(kt):
            o = acc if k == 0 else sq[k % 2]
            s = act(o[:], x[:, k, :], ACT.Square, *marks, freed[k % 2])
            if k:
                m = freed[k % 2] = tt(V, acc[:], acc[:], sq[k % 2][:], ALU.add, s, m)
            else:
                m = s

        def sums(half):
            nb, ps, free = banks.take()
            return nb, ps, mm(ps[:], ones[:], acc[:, hs(half)], True, True, m, free)

        return inverse_rms(ctx, sums, dst, n, *marks)

    w_in, w_glu, w_out = a["w_in"][0], a["w_glu"][0], a["w_out"][0]
    w_gate, w_up, w_down = a["w_gate"][0], a["w_up"][0], a["w_down"][0]

    res = ExitStack()
    hT = sb(res, "hT", [P, KD, L])
    u_ctx = ExitStack()
    u_pool = sb(u_ctx, "u_pool", [P, 4, L])
    u_tok = sb(u_ctx, "u_tok", [P, SG, SJ, SH])
    rs_col = sb(u_ctx, "rs_col", [P, SJ])

    with ExitStack() as ctx:
        x_tok = sb(ctx, "x_tok", [P, SJ, D])
        junk = sb(ctx, "junk", [P, D])
        c_x = [count(f"x_in{i}") for i in range(2)]
        x_view = a["x"][0].rearrange("(c j) d -> c j d", j=SJ)
        hT_view = hT[:].rearrange("p k (c j) -> p k j c", j=SJ)
        for part in range(2):
            js = slice(part * 4, part * 4 + 4)
            Q.dma(c_x[part], x_tok[:, js, :], x_view[:, js, :])
        for j in range(SJ):
            x_here = (c_x[j // 4], 16)
            m = S.do(lambda e, j=j: e.activation(junk[:], x_tok[:, j, :], ACT.Square,
                                                 accum_out=rs_col[:, j:j + 1]), x_here)
        m = act(rs_col[:], rs_col[:], ACT.Sqrt, m, bias=eps_col, scale=1.0 / D)
        rs_col_ready = V.do(lambda e: e.reciprocal(rs_col[:], rs_col[:]), m)
        n_ev = 0
        for part in range(2):
            for k in range(KD):
                n, ps, free = banks.take()
                for i in range(4):
                    j = part * 4 + i
                    m = transpose(ps[:, i * P:(i + 1) * P], x_tok[:, j, k * P:(k + 1) * P],
                                  (c_x[part], 16), free)
                n_ev += 1
                m = copy(evac_engine(n_ev), hT_view[:, k, part * 4:part * 4 + 4, :],
                         ps[:].rearrange("p (j c) -> p j c", j=4), m)
                banks.release(n, m)
        rs_view = rs[:].rearrange("p (c j) -> p j c", j=SJ)
        for part in range(2):
            n, ps, free = banks.take()
            for i in range(4):
                j = part * 4 + i
                m = mm(ps[:, i * P:(i + 1) * P], rs_col[:, j:j + 1].to_broadcast([P, P]), ident[:],
                       True, True, rs_col_ready, free)
            m = copy(V, rs_view[:, part * 4:part * 4 + 4, :], ps[:].rearrange("p (j c) -> p j c", j=4), m)
            banks.release(n, m)
    fence()

    with ExitStack() as ctx:
        weights = Weights(ctx, [wblock(w_in, 0, KD, 256 * i, 256) for i in range(4)])
        hi = sb(ctx, "hg_hi", [P, KD, L], F32R)
        lo = sb(ctx, "hg_lo", [P, KD, L], F32R)
        ready = split_scaled(hT, vec["norm_mix"], hi, lo)

        def to_pool(i, half, ps, m):
            return [tt(V, u_pool[:, i, hs(half)], ps[:], rs[:, hs(half)], ALU.mult, m)]

        for b in range(2):
            linear(weights, (hi, lo), KD, [(0, 2 * b), (P, 2 * b + 1)], to_pool, ready)
        tok = [t[:].rearrange("p k (c j) -> p k j c", j=SJ) for t in (hi, lo)]
        for b in range(2):
            whi, wlo, there = weights.take()
            for j in range(SJ):
                n, ps, free = banks.take()
                pairs = []
                for k in range(KD):
                    pairs += [(tok[0][:, k, j, :], whi[:, k, :]), (tok[0][:, k, j, :], wlo[:, k, :]),
                              (tok[1][:, k, j, :], whi[:, k, :])]
                last = product(ps[:, 0:256], pairs, free, there, ready)
                o = u_tok[:, 16 * b:16 * b + 16, j, :]
                i_ = ps[:, 0:256].rearrange("p (g h) -> p g h", h=SH)
                m = act(o, i_, ACT.Copy, last, scale=rs_col[:, j:j + 1])
                banks.release(n, m)
            weights.done(last)
    fence()

    def sincos(sin_o, cos_o, theta, tmp, *marks):
        t, r = tmp
        c1 = 6.28125
        c2 = float(np.float32((TWO_PI - c1) // 2.0 ** -20 * 2.0 ** -20))
        c3 = TWO_PI - c1 - c2
        ts(V, t, theta, 1.0 / TWO_PI, MAGIC, ALU.mult, ALU.add, *marks)
        ts(V, t, t, -MAGIC, None, ALU.add, None)
        stt(r, t, -c1, theta, ALU.mult, ALU.add)
        stt(r, t, -c2, r, ALU.mult, ALU.add)
        stt(r, t, -c3, r, ALU.mult, ALU.add)
        top = float(np.float32(3.1415925))
        m = ts(V, r, r, top, -top, ALU.min, ALU.max)
        m2 = act(sin_o, r, ACT.Sin, m)
        m3 = act(t, r, ACT.Sin, m, scale=0.5)
        m4 = tt(V, t, t, t, ALU.mult, m3)
        return ts(V, cos_o, t, -2.0, 1.0, ALU.mult, ALU.add, m4), m2

    def cmul(o, x, y, tmp, *marks):
        tt(V, tmp, x[1], y[1], ALU.mult, *marks)
        tt(V, o[0], x[0], y[0], ALU.mult)
        tt(V, o[0], o[0], tmp, ALU.subtract)
        tt(V, tmp, x[1], y[0], ALU.mult)
        tt(V, o[1], x[0], y[1], ALU.mult)
        return tt(V, o[1], o[1], tmp, ALU.add)

    y_ctx = ExitStack()
    y_tok = sb(y_ctx, "y_tok", [P, SJ, SG, SH])
    with ExitStack() as ctx:
        c_s = count("ssm_params_in")
        lam_rows = sb(ctx, "lam_rows", [SG, 4, SP_])
        dt = sb(ctx, "dt", [P, SG])
        bx = sb(ctx, "bx", [P, SG, SH])
        by = sb(ctx, "by", [P, SG, SH])
        c_rows = sb(ctx, "c_rows", [P, 4, 2, P])
        d_row = sb(ctx, "d_row", [P, SG * SH])
        swap = sb(ctx, "swap", [P, P])
        re, im = (a[n][0] for n in ("lam_re", "lam_im"))
        b_re, b_im = (a[n][0].rearrange("g p h -> p g h") for n in ("b_re", "b_im"))
        c_re, c_im = (a[n][0].rearrange("g h p -> (g h) p").rearrange("(n r) p -> r n p", r=P)
                      for n in ("c_re", "c_im"))
        for i, w in enumerate((re, re, im, im)):
            Q.dma(c_s, lam_rows[:, i, :], w)
        Q.dma(c_s, dt[:], a["log_dt"].to_broadcast([P, SG]))
        for t, top, bottom in ((bx, b_re, b_im), (by, b_im, b_re)):
            Q.dma(c_s, t[0:64], top)
            Q.dma(c_s, t[64:128], bottom)
        for i, (left, right) in enumerate(((c_re, c_im), (c_im, c_re))):
            Q.dma(c_s, c_rows[:, :, i, 0:64], left)
            Q.dma(c_s, c_rows[:, :, i, 64:128], right)
        Q.dma(c_s, d_row[:], a["d_skip"][0].rearrange("(a g) h -> a (g h)", a=1).to_broadcast([P, SG * SH]))
        here = Q.dma(c_s, swap[:], a["k_swap"])

        n, ps, free = banks.take()
        m = transpose(ps[:, 0:SG], lam_rows[:, 0:2, :].rearrange("g a p -> g (a p)"), here, free)
        m = transpose(ps[:, SG:2 * SG], lam_rows[:, 2:4, :].rearrange("g a p -> g (a p)"), here, free)
        lam = sb(ctx, "lam", [P, 2, SG])
        m = copy(V, lam[:], ps[:, 0:2 * SG].rearrange("p (a g) -> p a g", a=2), m)
        banks.release(n, m)
        lr, li = lam[:, 0, :], lam[:, 1, :]
        small = lambda name: sb(ctx, name, [P, SG])
        mag, r8, theta, tmp1, tmp2, sn, cs = (small(n_) for n_ in
                                              ("mag", "r8", "theta", "tmp1", "tmp2", "sn", "cs"))
        m = act(dt[:], dt[:], ACT.Exp, here)
        tt(V, theta[:], li, dt[:], ALU.mult, m)
        m = tt(V, tmp1[:], lr, dt[:], ALU.mult)
        act(mag[:], tmp1[:], ACT.Exp, m)
        m = act(r8[:], tmp1[:], ACT.Exp, m, scale=float(SJ))
        m = sincos(sn[:], cs[:], theta[:], (tmp1[:], tmp2[:]), m)
        pw = sb(ctx, "pw", [P, 2, SJ + 1, SG])
        V.do(lambda e: e.memset(pw[:, 0, 0, :], 1.0))
        V.do(lambda e: e.memset(pw[:, 1, 0, :], 0.0))
        tt(V, pw[:, 0, 1, :], mag[:], cs[:], ALU.mult, *m)
        tt(V, pw[:, 1, 1, :], mag[:], sn[:], ALU.mult)
        for i in range(2, SJ + 1):
            cmul((pw[:, 0, i, :], pw[:, 1, i, :]), (pw[:, 0, i - 1, :], pw[:, 1, i - 1, :]),
                 (pw[:, 0, 1, :], pw[:, 1, 1, :]), tmp1[:])
        den, nr, cf = small("den"), small("nr"), sb(ctx, "cf", [P, 2, SG])
        tt(V, den[:], lr, lr, ALU.mult)
        tt(V, tmp1[:], li, li, ALU.mult)
        tt(V, den[:], den[:], tmp1[:], ALU.add)
        V.do(lambda e: e.reciprocal(den[:], den[:]))
        ts(V, nr[:], pw[:, 0, 1, :], -1.0, None, ALU.add, None)
        ni = pw[:, 1, 1, :]
        for i, (p_, q_, op) in enumerate((((nr[:], lr), (ni, li), ALU.add), ((ni, lr), (nr[:], li), ALU.subtract))):
            tt(V, cf[:, i, :], *p_, ALU.mult)
            tt(V, tmp1[:], *q_, ALU.mult)
            tt(V, cf[:, i, :], cf[:, i, :], tmp1[:], op)
            tt(V, cf[:, i, :], cf[:, i, :], den[:], ALU.mult)
        gains = sb(ctx, "gains", [P, 2, SG, SJ])
        for s_ in range(SJ):
            m_gains = cmul((gains[:, 0, :, s_], gains[:, 1, :, s_]),
                           (pw[:, 0, SJ - 1 - s_, :], pw[:, 1, SJ - 1 - s_, :]), (cf[:, 0, :], cf[:, 1, :]),
                           tmp1[:])
        turn = sb(ctx, "turn", [P, 2, 8, SG])
        copy(V, turn[:, 0, 0, :], cs[:])
        ts(V, turn[:, 1, 0, :], sn[:], sign_pm, None, ALU.mult, None)
        for k in range(3):
            cmul((tmp2[:], nr[:]), (turn[:, 0, 0, :], turn[:, 1, 0, :]), (turn[:, 0, 0, :], turn[:, 1, 0, :]),
                 tmp1[:])
            copy(V, turn[:, 0, 0, :], tmp2[:])
            copy(V, turn[:, 1, 0, :], nr[:])
        for k in range(1, 7):
            cmul((turn[:, 0, k, :], turn[:, 1, k, :]), (turn[:, 0, k - 1, :], turn[:, 1, k - 1, :]),
                 (turn[:, 0, k - 1, :], turn[:, 1, k - 1, :]), tmp1[:])
        ts(V, by[:], by[:], sign_mp, None, ALU.mult, None)
        cx = sb(ctx, "cx", [P, SG, SH])
        cy = sb(ctx, "cy", [P, SG, SH])
        for i, (t, sign) in enumerate(((cx, sign_pm), (cy, minus_one))):
            n, ps, free = banks.take()
            for q in range(4):
                m = transpose(ps[:, q * P:(q + 1) * P], c_rows[:, q, i, :], here, free)
            m_c = ts(V, t[:].rearrange("p g h -> p (g h)"), ps[:], sign, None, ALU.mult, None, m)
            banks.release(n, m_c)

        lead = sb(ctx, "lead", [P, GB, 2 * SJ - 1, SH])
        m_lead0 = G.do(lambda e: e.memset(lead[:], 0.0))
        tmp = sb(ctx, "tmp", [P, GB * SC])
        ca = sb(ctx, "ca", [P, GB, SJ, SH])
        state_in = [sb(ctx, "state_in", [P, GB, P]) for _ in range(2)]
        toep = sb(ctx, "toep", [P, GB, P])
        u_rows = sb(ctx, "u_rows", [P, GB, SC])
        phase = sb(ctx, "phase", [P, 2, GB, SC])
        step = sb(ctx, "step", [P, GB, SC])
        z = sb(ctx, "z", [P, GB, SC])
        state = sb(ctx, "state", [P, GB, SC + 1])
        m_zero = G.do(lambda e: e.memset(state[:], 0.0))
        du = sb(ctx, "du", [P, SJ, SG, SH])
        m_du = None
        for j in range(SJ):
            m_du = tt(G, du[:, j, :, :], u_tok[:, :, j, :],
                      d_row[:].rearrange("p (g h) -> p g h", h=SH), ALU.mult, here)
        m_state_read = m_toep_read = m_u_read = m_ca_read = None
        for b in range(SG // GB):
            gs = slice(b * GB, b * GB + GB)
            shape = [P, GB, SJ, SH]
            over_h = lambda v: v.unsqueeze(3).to_broadcast(shape)
            over_j = lambda v: v.unsqueeze(2).to_broadcast(shape)
            tview = tmp[:, 0:GB * SJ * SH].rearrange("p (g j h) -> p g j h", g=GB, j=SJ)
            pv = lambda i: pw[:, i, 1:SJ + 1, gs].rearrange("p j g -> p g j")
            tt(V, lead[:, :, 0:SJ, :], over_h(gains[:, 0, gs, :]), over_j(bx[:, gs, :]), ALU.mult,
               m_lead0, m_toep_read)
            tt(V, tview, over_h(gains[:, 1, gs, :]), over_j(by[:, gs, :]), ALU.mult)
            m_lead = tt(V, lead[:, :, 0:SJ, :], lead[:, :, 0:SJ, :], tview, ALU.add)
            tt(V, ca[:], over_h(pv(0)), over_j(cx[:, gs, :]), ALU.mult, m_ca_read)
            tt(V, tview, over_h(pv(1)), over_j(cy[:, gs, :]), ALU.mult)
            m_ca = tt(V, ca[:], ca[:], tview, ALU.add)
            for q in range(2):
                n, ps, free = banks.take()
                for i in range(4):
                    g = b * GB + q * 4 + i
                    m = transpose(ps[:, i * P:(i + 1) * P], u_tok[:, g, :, :].rearrange("p j h -> p (j h)"),
                                  free)
                m_u = copy(S, u_rows[:, q * 4:q * 4 + 4, :], ps[:].rearrange("p (g c) -> p g c", g=4), m,
                           m_u_read)
                banks.release(n, m_u)
            for q in range(2):
                n, ps, free = banks.take()
                for i in range(4):
                    m = transpose(ps[:, i * P:(i + 1) * P],
                                  lead[:, q * 4 + i, 0:SJ, :].rearrange("p s h -> p (s h)"), m_lead, free)
                v = ps[:].rearrange("p (g a q) -> p g a q", g=4, a=2)
                o = [t[:, q * 4:q * 4 + 4, :].rearrange("p g (a q) -> p g a q", a=2) for t in state_in]
                copy(V, o[0], v, m, m_state_read)
                copy(V, o[1][:, :, 0, :], v[:, :, 1, :])
                m_in = copy(V, o[1][:, :, 1, :], v[:, :, 0, :])
                banks.release(n, m_in)
            for q in range(2):
                n, ps, free = banks.take()
                for i in range(4):
                    for j in range(SJ):
                        lag = lead[:, q * 4 + i, SJ - 1 - j:2 * SJ - 1 - j, :].rearrange("p s h -> p (s h)")
                        m = mm(ps[:, i * P + j * SH:i * P + (j + 1) * SH], lag, cx[:, b * GB + q * 4 + i, :],
                               True, True, m_lead, m_c, free)
                m_toep_read = m
                m_toep = copy(S, toep[:, q * 4:q * 4 + 4, :], ps[:].rearrange("p (g n) -> p g n", g=4), m,
                              m_u_read)
                banks.release(n, m_toep)
            V.do(lambda e: e.memset(phase[:, 0, :, 0:1], 1.0))
            V.do(lambda e: e.memset(phase[:, 1, :, 0:1], 0.0))
            for k in range(7):
                w = 1 << k
                by_turn = lambda i: turn[:, i, k, gs].unsqueeze(2).to_broadcast([P, GB, w])
                cmul((phase[:, 0, :, w:2 * w], phase[:, 1, :, w:2 * w]),
                     (phase[:, 0, :, 0:w], phase[:, 1, :, 0:w]), (by_turn(0), by_turn(1)),
                     tmp[:, 0:GB * w].rearrange("p (g w) -> p g w", g=GB))
            m_phase = copy(V, step[:], r8[:, gs].unsqueeze(2).to_broadcast([P, GB, SC]))
            V.do(lambda e: e.memset(step[:, :, 0:1], 0.0))
            tm = tmp[:].rearrange("p (g c) -> p g c", g=GB)
            for q in range(2):
                qs = slice(q * 4, q * 4 + 4)
                both = []
                for s_ in range(2):
                    n, ps, free = banks.take()
                    for i in range(4):
                        m = mm(ps[:, i * P:(i + 1) * P], state_in[s_][:, q * 4 + i, :],
                               u_rows[:, q * 4 + i, :], True, True, m_in, m_u, free)
                    both.append((n, ps, m))
                m_state_read = m
                flat = lambda v: v.rearrange("p g c -> p (g c)")
                m1 = tt(V, flat(z[:, qs, :]), flat(phase[:, 0, qs, :]), both[0][1][:], ALU.mult, both[0][2])
                m2 = tt(V, flat(tm[:, qs, :]), flat(phase[:, 1, qs, :]), both[1][1][:], ALU.mult, both[1][2])
                banks.release(both[0][0], m1)
                banks.release(both[1][0], m2)
            fz, fm = flat(z[:]), flat(tm)
            tt(V, fz, fz, fm, ALU.add)
            m_z = V.do(lambda e: e.tensor_tensor_scan(fz, flat(step[:]), fz, 0.0, ALU.mult, ALU.add))
            for q in range(2):
                qs = slice(q * 4, q * 4 + 4)
                n, ps, free = banks.take()
                m = mm(ps[:], swap[:], flat(z[:, qs, :]), True, True, m_z, free)
                m1 = tt(V, flat(tm[:, qs, :]), flat(phase[:, 1, qs, :]), ps[:], ALU.mult, m)
                banks.release(n, m1)
            tt(V, fz, fz, flat(phase[:, 0, :, :]), ALU.mult)
            m_state = tt(V, state[:, :, 1:SC + 1], z[:], tm, ALU.subtract, m_ca_read, m_zero)
            for q in range(2):
                n, ps, free = banks.take()
                for i in range(4):
                    g = q * 4 + i
                    o = ps[:, i * P:(i + 1) * P]
                    mm(o, u_rows[:, g, :], toep[:, g, :], True, False, m_toep, free)
                    m = mm(o, state[:, g, 0:SC], ca[:, g, :, :].rearrange("p j h -> p (j h)"), False, True,
                           m_state, m_ca)
                m_u_read = m_ca_read = m
                m1 = V.do(lambda e, o=y_tok[:, :, b * GB + q * 4:b * GB + q * 4 + 4, :],
                          i_=ps[:].rearrange("p (g j h) -> p j g h", g=4, j=SJ): e.tensor_copy(o, i_), m)
                banks.release(n, m1)
        m = tt(V, y_tok[:].rearrange("p j g h -> p (j g h)"), y_tok[:].rearrange("p j g h -> p (j g h)"),
               du[:].rearrange("p j g h -> p (j g h)"), ALU.add, m_du)
        for j in range(SJ):
            y_j = y_tok[:, j, :, :].rearrange("p g h -> p (g h)")
            m_gelu = act(y_j, y_j, ACT.Gelu_apprx_tanh, m)
    fence()
    mix = ExitStack()
    y_hi = sb(mix, "y_hi", [P, KD, L], F32R)
    y_lo = sb(mix, "y_lo", [P, KD, L], F32R)
    with ExitStack() as ctx:
        weights = Weights(ctx, [wblock(w_glu, 0, 4, 0, 512)], raw=1, parts=1)
        yT = u_tok[:].rearrange("p g j h -> p (g j h)").rearrange("p (k t) -> p k t", k=4)
        g_hi = sb(ctx, "g_hi", [P, 4, HALF], F32R)
        g_lo = sb(ctx, "g_lo", [P, 4, HALF], F32R)
        yT_view = yT.rearrange("p k (c j) -> p k j c", j=SJ)
        y_ready = []
        for k in range(4):
            for part in range(2):
                n, ps, free = banks.take()
                for i in range(4):
                    m = transpose(ps[:, i * P:(i + 1) * P],
                                  y_tok[:, part * 4 + i, 8 * k:8 * k + 8, :].rearrange("p g h -> p (g h)"),
                                  free)
                m = copy(evac_engine(part), yT_view[:, k, part * 4:part * 4 + 4, :],
                         ps[:].rearrange("p (j c) -> p j c", j=4), m)
                banks.release(n, m)
                y_ready.append(m)
        whi, wlo, there = weights.take()
        gate = sb(ctx, "gate", [P, 2, HALF])
        gated = sb(ctx, "gated", [P, 2, HALF])
        m_read, gate_free = None, [None, None]
        for half in range(2):
            for k in range(4):
                m1 = act(g_hi[:, k, :], yT[:, k, hs(half)], ACT.Copy, y_ready, m_read)
                m_split = tt(V, g_lo[:, k, :], yT[:, k, hs(half)], g_hi[:, k, :], ALU.subtract, m1, m_read,
                             y_ready)
            for i in range(4):
                n, ps, free = banks.take()
                m_read = product(ps[:], three((whi, wlo), (g_hi, g_lo), 4, slice(i * P, (i + 1) * P),
                                              slice(0, HALF)), free, there, m_split)
                b = i % 2
                m = act(gate[:, b, :], ps[:], ACT.Sigmoid, m_read, gate_free[b], bias=vec["b_glu"][:, i:i + 1])
                banks.release(n, m)
                m = tt(V, gated[:, b, :], gate[:, b, :], yT[:, i, hs(half)], ALU.mult, m)
                m1 = act(y_hi[:, 4 + i, hs(half)], gated[:, b, :], ACT.Copy, m)
                gate_free[b] = tt(V, y_lo[:, 4 + i, hs(half)], gated[:, b, :], y_hi[:, 4 + i, hs(half)],
                                  ALU.subtract, m1)
        weights.done(m_read)

        c_pool = count("pool_in")
        w_pool = sb(ctx, "w_pool", [P, 4, P])
        inv_n = sb(ctx, "inv_n", [P, 4, 16])
        Q.dma(c_pool, inv_n[:].rearrange("p w n -> p (w n)"), a["k_pool"])
        pool_here = Q.dma(c_pool, w_pool[:], a["w_pool"][0].rearrange("g c d -> c g d"))
        y_flat = y_tok[:].rearrange("p j g h -> p (j g h)")
        sums = [y_flat[:, 0:L], y_flat[:, L:2 * L]]
        G.wait(y_ready)
        for i, w in enumerate(WINDOWS):
            src = u_pool[:, i, :]
            lag, b = 1, 0
            while lag < w:
                dst = sums[b]
                m = copy(G, dst[:, 0:lag], src[:, 0:lag])
                m = tt(G, dst[:, lag:L], src[:, lag:L], src[:, 0:L - lag], ALU.add)
                src, lag, b = dst, 2 * lag, 1 - b
            m1 = tt(V, src[:, 0:16], src[:, 0:16], inv_n[:, i, :], ALU.mult, m, pool_here)
            m1 = ts(V, src[:, 16:L], src[:, 16:L], 1.0 / w, None, ALU.mult, None)
            m_d = tt(V, u_pool[:, i, :], src, u_pool[:, i, :], ALU.subtract, m1)
            G.wait(m_d)
            scale = vec["pool_scale"][:, i:i + 1]
            for half in range(2):
                n, ps, free = banks.take()
                m = mm(ps[:], w_pool[:, i, :], u_pool[:, i, hs(half)], True, True, m_d, free, pool_here)
                m1 = act(y_hi[:, i, hs(half)], ps[:], ACT.Copy, m, scale=scale)
                m2 = stt(y_lo[:, i, hs(half)], ps[:], scale, y_hi[:, i, hs(half)], ALU.mult, ALU.subtract, m1)
                banks.release(n, m1, m2)
    fence()

    def to_residual(i, half, ps, m):
        return [tt(V, hT[:, i, hs(half)], hT[:, i, hs(half)], ps[:], ALU.add, m)]

    with ExitStack() as ctx:
        weights = Weights(ctx, [wblock(w_out, 0, KD, 256 * i, 256) for i in range(4)])
        for b in range(4):
            linear(weights, (y_hi, y_lo), KD, [(0, 2 * b), (P, 2 * b + 1)], to_residual, None)
    fence()
    mix.close()
    y_ctx.close()
    u_ctx.close()

    FC = 4

    def ffn_chunks(d_ff):
        n_t = d_ff // P
        return [(t0, min(FC, n_t - t0)) for t0 in range(0, n_t, FC)]

    def split_to(fh, fl, f, i, half, m, free):
        m1 = act(fh[:, i, hs(half)], f, ACT.Copy, m, free)
        return m1, tt(G, fl[:, i, hs(half)], f, fh[:, i, hs(half)], ALU.subtract, m1, m, free)

    def down(weights, parts, nt, ready):
        for _ in range(2):
            hi_, lo_, there = weights.take()
            for i in range(4):
                for half in range(2):
                    n, ps, free = banks.take()
                    last = product(ps[:], three((hi_, lo_), parts, nt, slice(i * P, (i + 1) * P), hs(half)),
                                   free, there, ready)
                    banks.release(n, *to_residual(_ * 4 + i, half, ps, last))
            weights.done(last)
        return last

    if True:
        with ExitStack() as ctx:
            rs_ready = norm(ctx, hT, KD, rs, D)
        fence()
        with ExitStack() as ctx:
            plan = []
            for t0, nt in ffn_chunks(DFF):
                for q in range(0, nt, 2):
                    plan += [wblock(w_, 0, KD, (t0 + q) * P, 256) for w_ in (w_gate, w_up)]
                plan += [wblock(w_down, t0 * P, nt, i * 512, 512) for i in range(2)]
            weights = Weights(ctx, plan)
            hi = sb(ctx, "hf_hi", [P, KD, L], F32R)
            lo = sb(ctx, "hf_lo", [P, KD, L], F32R)
            f_hi = sb(ctx, "f_hi", [P, FC, L], F32R)
            f_lo = sb(ctx, "f_lo", [P, FC, L], F32R)
            gates = sb(ctx, "gates", [P, 4, HALF])
            gate_ready, gate_free = [None] * 4, [None] * 4
            f_tmp = sb(ctx, "f_tmp", [P, 2, HALF])
            f_free = [None, None]
            ready = split_scaled(hT, vec["norm_ffn"], hi, lo)
            S.wait(rs_ready), V.wait(rs_ready)
            f_read, marks = None, []

            def to_gate(i, half, ps, m):
                s_ = (i % 2) * 2 + half
                m = tt(V, gates[:, s_, :], ps[:], rs[:, hs(half)], ALU.mult, m, gate_free[s_])
                gate_ready[s_] = act(gates[:, s_, :], gates[:, s_, :], ACT.Silu, m)
                return [m]

            def to_hidden(i, half, ps, m):
                s_ = (i % 2) * 2 + half
                t = f_tmp[:, half, :]
                m = tt(V, t, ps[:], rs[:, hs(half)], ALU.mult, m, f_free[half])
                m1 = gate_free[s_] = tt(V, t, t, gates[:, s_, :], ALU.mult, gate_ready[s_])
                f_free[half] = list(split_to(f_hi, f_lo, t, i, half, m1, f_read))
                marks.extend(f_free[half])
                return [m]

            for t0, nt in ffn_chunks(DFF):
                marks = []
                for q in range(0, nt, 2):
                    linear(weights, (hi, lo), KD, [(0, q), (P, q + 1)], to_gate, ready)
                    linear(weights, (hi, lo), KD, [(0, q), (P, q + 1)], to_hidden, ready)
                f_read = down(weights, (f_hi, f_lo), nt, marks)
        fence()
    w_in2, w_out2 = a["w_in_2"][0], a["w_out_2"][0]
    Z_KPE, Z_RWKV, Z_GATE = QLORA + KVLORA, QLORA + KVLORA + P, QLORA + KVLORA + P + RWKV_COLS

    def z_tile(row, half=None):
        t = z_dram[row:row + P, :]
        return t if half is None else t[:, hs(half)]

    with ExitStack() as ctx:
        ready = norm(ctx, hT, KD, rs, D)
        for k in range(KD):
            m = stt(hT[:, k, :], hT[:, k, :], vec["norm_final"][:, k:k + 1], rs[:], ALU.mult, ALU.mult, ready)
        x_kept = Q.dma(count("x_keep"), x_dram.rearrange("(k p) t -> p k t", p=P), hT[:], m)
        S.wait(m)
        rs_ready = norm(ctx, hT, KD, rs, D, m)
    fence()

    with ExitStack() as ctx:
        w3 = lambda c0, n: w_in2[:, c0:c0 + n].rearrange("(k p) c -> p k c", p=P)
        kpe0 = QLORA + KVLORA
        plan = [wblock(w_in2, 0, KD, 0, 256), wblock(w_in2, 0, KD, 256, 256),
                (KD, 256, [(0, w3(512, P))] + [piece for c0 in (128, 192) for piece in (
                    (c0, w3(kpe0, QR)), (c0 + 32, w3(kpe0 + 16, 16)), (c0 + 48, w3(kpe0, 16)))])]
        plan += [wblock(w_in2, 0, KD, MLA_COLS + 256 * i, 256) for i in range(RWKV_COLS // 256)]
        plan += [wblock(w_in2, 0, KD, MLA_COLS + RWKV_COLS + 256 * i, 256) for i in range(8)]
        weights = Weights(ctx, plan)
        hi = sb(ctx, "hz_hi", [P, KD, L], F32R)
        lo = sb(ctx, "hz_lo", [P, KD, L], F32R)
        store = Ring([sb(ctx, "z_out", [P, HALF]) for _ in range(6)], [count(f"z_out{i}") for i in range(6)])
        rows = [sb(ctx, "z_row", [P, L + 1]) for _ in range(2)]
        shifted = Ring([sb(ctx, "z_shift", [P, L]) for _ in range(2)], [count(f"zs_out{i}") for i in range(2)])
        for t in rows:
            V.do(lambda e, t=t: e.memset(t[:, 0:1], 0.0))
        ready = split_scaled(hT, vec["g_mix_2"], hi, lo)
        z_kept = []

        def to_z(i, half, ps, m):
            s_, t, free = store.take()
            m = tt(V, t[:], ps[:], rs[:, hs(half)], ALU.mult, m, free)
            kept = Q.dma(store.counts[s_], z_tile(i * P, half), t[:], m)
            store.release(s_, kept)
            return [m]

        def to_gates(i, half, ps, m):
            s_, t, free = store.take()
            m = tt(V, t[:], ps[:], rs[:, hs(half)], ALU.mult, m, free)
            m1 = act(t[:], t[:], ACT.Sigmoid, m)
            store.release(s_, Q.dma(store.counts[s_], z_tile(Z_GATE + i * P, half), t[:], m1))
            return [m]

        def to_rwkv(i, half, ps, m):
            row_, mu = rows[i % 2], vec["mu_rwkv_2"][:, i:i + 1]
            m = tt(V, row_[:, 1 + half * HALF:1 + half * HALF + HALF], ps[:], rs[:, hs(half)], ALU.mult, m)
            if half == 1:
                s_, t, free = shifted.take()
                tt(V, t[:], row_[:, 0:L], row_[:, 1:L + 1], ALU.subtract, free)
                m1 = stt(t[:], t[:], mu, row_[:, 1:L + 1], ALU.mult, ALU.add)
                shifted.release(s_, Q.dma(shifted.counts[s_], z_tile(Z_RWKV + i * P), t[:], m1))
            return [m]

        for b in range(3):
            linear(weights, (hi, lo), KD, [(0, 2 * b), (P, 2 * b + 1)], to_z, ready)
        for b in range(7):
            linear(weights, (hi, lo), KD, [(0, 2 * b), (P, 2 * b + 1)], to_rwkv, ready)
        for b in range(8):
            linear(weights, (hi, lo), KD, [(0, 2 * b), (P, 2 * b + 1)], to_gates, ready)
    res.close()
    fence()
    yw = ExitStack()
    y_wkv = sb(yw, "y_wkv", [P, NPAIR, L])
    heads = (slice(0, 64), slice(64, 128))
    with ExitStack() as ctx:
        c_rw = count("rwkv_in")
        ar = sb(ctx, "ar", [P, NPAIR, NC, 2, C])
        score_rb = sb(ctx, "score_rb", [P, NPAIR, NC, C])
        inv = sb(ctx, "inv", [P, NPAIR, NC, C])
        b_hat = sb(ctx, "b_hat", [P, NPAIR, NC, C])
        x_own = sb(ctx, "x_own", [P, NPAIR, NC, C])
        s_own = sb(ctx, "s_own", [P, NPAIR, NC, C])
        chunk_decay = sb(ctx, "chunk_decay", [P, NPAIR, NC])
        c_n = [count(f"n_out{i}") for i in range(NPAIR)]
        with ExitStack() as tctx:
            lo_rank = sb(tctx, "lo_rank", [P, L])
            g_rank = sb(tctx, "g_rank", [P, L])
            w2a2 = sb(tctx, "w2a2", [P, 512])
            g2 = sb(tctx, "g2", [P, 512])
            wkv_mask = sb(tctx, "wkv_mask", [P, 2 * C])
            chunk_mask = sb(tctx, "chunk_mask", [P, L])
            Q.dma(c_rw, lo_rank[:], z_tile(Z_RWKV + 1536))
            Q.dma(c_rw, g_rank[:], z_tile(Z_RWKV + 1664))
            Q.dma(c_rw, w2a2[0:64, :], a["w2_2"][0])
            Q.dma(c_rw, w2a2[64:128, :], a["a2_2"][0])
            Q.dma(c_rw, g2[:], a["g2_2"][0])
            Q.dma(c_rw, wkv_mask[:], a["k_wkv_mask"])
            here = Q.dma(c_rw, chunk_mask[:], a["k_chunk_mask"])
            m = act(lo_rank[0:64, :], lo_rank[0:64, :], ACT.Tanh, here)
            ranks = act(g_rank[:], g_rank[:], ACT.Sigmoid, m)
            tile = lambda name: sb(tctx, name, [P, L])
            r_, k_, v_ = tile("r"), tile("k"), tile("v")
            sg, cs, ea, eb, a_, kk, t1, t2 = (tile(n_) for n_ in ("sg", "cs", "ea", "eb", "a", "kk", "t1", "t2"))
            k_score = sb(tctx, "k_score", [P, NC // 2, 2, C])
            c_p = [count(f"pair_in{i}") for i in range(3)]
            c_o = [count(f"pair_out{i}") for i in range(2)]
            by_chunk = lambda t: t[:].rearrange("p (c t) -> p c t", t=C)
            for p in range(NPAIR):
                pc = slice(p * P, (p + 1) * P)
                col = lambda name: vec[name][:, p:p + 1]
                before = [(s_.done, s_.done.value) for s_ in (V, S, G, T)] + \
                    [(c_, c_.value) for c_ in c_o] if p else []
                r_here = Q.dma(c_p[0], r_[:], z_tile(Z_RWKV + p * P), *before)
                k_here = Q.dma(c_p[1], k_[:], z_tile(Z_RWKV + 512 + p * P))
                v_here = Q.dma(c_p[2], v_[:], z_tile(Z_RWKV + 1024 + p * P))
                for half in range(2):
                    n, ps, free = banks.take()
                    m = mm(ps[:], w2a2[0:64, pc], lo_rank[0:64, hs(half)], True, True, ranks, free)
                    banks.release(n, act(sg[:, hs(half)], ps[:], ACT.Sigmoid, m, *before, bias=col("w0_2")))
                    n, ps, free = banks.take()
                    m = mm(ps[:], w2a2[64:128, pc], lo_rank[64:128, hs(half)], True, True, free)
                    m_a = act(a_[:, hs(half)], ps[:], ACT.Sigmoid, m, *before, bias=col("a0_2"))
                    banks.release(n, m_a)
                    n, ps, free = banks.take()
                    m = mm(ps[:], g2[:, pc], g_rank[:, hs(half)], True, True, free)
                    m_g = copy(S, t2[:, hs(half)], ps[:], m)
                    banks.release(n, m_g)
                g_out = Q.dma(c_o[0], g_dram[pc, :], t2[:], m_g)
                ts(V, kk[:], k_[:], col("k_k_2"), None, ALU.mult, None, k_here, *before)
                m = tt(V, t1[:], kk[:], kk[:], ALU.mult)
                for half in range(2):
                    n, ps, free = banks.take()
                    m1 = mm(ps[:], headones[:], t1[:, hs(half)], True, True, m, free)
                    m2 = act(eb[:, hs(half)], ps[:], ACT.Sqrt, m1)
                    banks.release(n, m2)
                ts(V, eb[:], eb[:], 1e-12, None, ALU.max, None, m2)
                V.do(lambda e: e.reciprocal(eb[:], eb[:]))
                m_kk = tt(V, kk[:], kk[:], eb[:], ALU.mult)
                ts(V, t1[:], a_[:], -1.0, col("k_a_2"), ALU.add, ALU.mult, m_a)
                stt(k_[:], t1[:], 1.0, k_[:], ALU.add, ALU.mult)
                m = stt(t1[:], r_[:], col("r_k_2"), k_[:], ALU.mult, ALU.mult, r_here)
                for half in range(2):
                    n, ps, free = banks.take()
                    m1 = mm(ps[:], headones[:], t1[:, hs(half)], True, True, m, free)
                    m2 = tt(V, t2[:, hs(half)], ps[:], v_[:, hs(half)], ALU.mult, m1, v_here, g_out)
                    banks.release(n, m2)
                bonus_out = Q.dma(c_o[1], bonus_dram[pc, :], t2[:], m2)
                m = V.do(lambda e: e.tensor_tensor_scan(cs[:], chunk_mask[:], sg[:], 0.0, ALU.mult, ALU.add), here,
                         (S.done, S.done.value))
                m1 = act(ea[:], cs[:], ACT.Exp, m, scale=-DECAY)
                m = tt(V, sg[:], cs[:], sg[:], ALU.subtract)
                m2 = act(eb[:], sg[:], ACT.Exp, m, m_kk, scale=-DECAY)
                at_view, rt_view = ar[:, p, :, 0, :], ar[:, p, :, 1, :]
                tt(V, rt_view, by_chunk(r_), by_chunk(ea), ALU.mult, m1)
                copy(V, chunk_decay[:, p, :], by_chunk(ea)[:, :, C - 1])
                m_ar = stt(at_view, by_chunk(kk), -1.0, by_chunk(eb), ALU.mult, ALU.mult, m2)
                m_kka = tt(V, kk[:], kk[:], a_[:], ALU.mult)
                m1 = act(ea[:], cs[:], ACT.Exp, m_ar, scale=DECAY)
                end = by_chunk(cs)[:, :, C - 1:C].to_broadcast([P, NC, C])
                m_e = tt(V, by_chunk(t1), by_chunk(cs), end, ALU.subtract, (T.done, T.done.value))
                m2 = act(eb[:], t1[:], ACT.Exp, m_e, m_ar, scale=DECAY)
                m_bt = tt(V, sg[:], kk[:], ea[:], ALU.mult, m1)
                m_kt = tt(V, cs[:], k_[:], ea[:], ALU.mult, m_e)
                m_bh = tt(V, a_[:], kk[:], eb[:], ALU.mult, m2)
                m_kh = tt(V, t1[:], k_[:], eb[:], ALU.mult)
                for src, dst, m_src in ((a_, b_hat[:, p, :, :], m_bh), (t1, by_chunk(ea), m_kh),
                                        (v_, by_chunk(eb), m_kh)):
                    for q in range(2):
                        n, ps, free = banks.take()
                        for i in range(8):
                            c = q * 8 + i
                            for h in heads:
                                m = mm(ps[h, i * C:(i + 1) * C], src[h, c * C:(c + 1) * C], ident[h, h],
                                       True, True, m_src, free, signal=(i == 7 and h is heads[1]))
                        m = copy(S, dst[:, q * 8:q * 8 + 8, :], ps[:].rearrange("p (c t) -> p c t", c=8), m)
                        banks.release(n, m)
                m_rows = m
                khs, vs = by_chunk(ea), by_chunk(eb)
                mask2 = wkv_mask[:].rearrange("p (a t) -> p a t", a=2)
                over_c = lambda v: v.unsqueeze(1).to_broadcast([P, 4, C])
                k_read = None
                for q in range(4):
                    n, ps, free = banks.take()
                    for i in range(4):
                        c = q * 4 + i
                        for h in heads:
                            m = mm(ps[h, i * P:(i + 1) * P], sg[h, c * C:(c + 1) * C],
                                   ar[h, p, c, :, :].rearrange("p a t -> p (a t)"), True, True, m_bt, m_ar, free,
                                   signal=(i == 3 and h is heads[1]))
                    v4 = ps[:].rearrange("p (c a t) -> p c a t", c=4, a=2)
                    cq = slice(q * 4, q * 4 + 4)
                    tt(V, inv[:, p, cq, :], v4[:, :, 0, :], over_c(mask2[:, 0, :]), ALU.mult, m)
                    m_n = tt(V, score_rb[:, p, cq, :], v4[:, :, 1, :], over_c(mask2[:, 1, :]), ALU.mult)
                    banks.release(n, m_n)
                n_view = n_dram.rearrange("(p h c) (s t) -> p h s c t", p=NPAIR, h=2, s=C)
                for i_h, h in enumerate(heads):
                    n_out = Q.dma(c_n[p], n_view[p, i_h], inv[h, p, :, :], m_n)
                for q8 in range(2):
                    for q in range(2):
                        n, ps, free = banks.take()
                        for i in range(4):
                            c = q8 * 8 + q * 4 + i
                            for h in heads:
                                m = mm(ps[h, i * P:(i + 1) * P], cs[h, c * C:(c + 1) * C],
                                       ar[h, p, c, :, :].rearrange("p a t -> p (a t)"), True, True, m_kt, m_ar,
                                       free, signal=(i == 3 and h is heads[1]))
                        m_ks = V.do(lambda e, o=k_score[:, q * 4:q * 4 + 4, :, :].rearrange("p c a t -> p c (a t)"),
                                    x=ps[:].rearrange("p (c n) -> p c n", c=4),
                                    y=wkv_mask[:].unsqueeze(1).to_broadcast([P, 4, P]):
                                    e.tensor_tensor(o, x, y, ALU.mult), m, k_read)
                        banks.release(n, m_ks)
                    c8 = slice(q8 * 8, q8 * 8 + 8)
                    for kind in range(3):
                        n, ps, free = banks.take()
                        for i in range(8):
                            c = q8 * 8 + i
                            for h in heads:
                                w, x = ((k_score[h, i, 0, :], vs[h, c, :]), (vs[h, c, :], k_score[h, i, 1, :]),
                                        (khs[h, c, :], vs[h, c, :]))[kind]
                                m = mm(ps[h, i * C:(i + 1) * C], w, x, True, True, m_ks, m_rows, free,
                                       signal=(i == 7 and h is heads[1]))
                        dst = (x_own[:, p, c8, :], y_wkv[:, p, q8 * HALF:(q8 + 1) * HALF].rearrange(
                            "p (c t) -> p c t", c=8), s_own[:, p, c8, :])[kind]
                        m1 = copy(S, dst, ps[:].rearrange("p (c t) -> p c t", c=8), m)
                        banks.release(n, m1)
                    k_read = m
        fence()

        with ExitStack() as tctx:
            nu = sb(tctx, "nu", [P, C, C])
            ru = sb(tctx, "ru", [P, C, C])
            tmp_v = sb(tctx, "tmp_v", [P, C * C // 4])
            c_u = count("units")
            here = Q.dma(c_u, nu[:].rearrange("p s t -> p (s t)"), n_dram)
            V.do(lambda e: e.memset(ru[:], 0.0))
            m = V.do(lambda e: e.memset(ru[:].rearrange("p s t -> p (s t)")[:, 0:C * C:C + 1], 1.0), here)
            for s_ in range(C - 1):
                i_n, t_n = s_ + 1, C - 1 - s_
                shape = [P, i_n, t_n]
                tv = tmp_v[:, 0:i_n * t_n].rearrange("p (i t) -> p i t", i=i_n)
                tt(V, tv, ru[:, 0:i_n, s_:s_ + 1].to_broadcast(shape),
                   nu[:, s_:s_ + 1, s_ + 1:C].to_broadcast(shape), ALU.mult)
                m = tt(V, ru[:, 0:i_n, s_ + 1:C], ru[:, 0:i_n, s_ + 1:C], tv, ALU.add)
            r_out = Q.dma(c_u, r_dram, ru[:].rearrange("p s t -> p (s t)"), m)
            r_view = r_dram.rearrange("(p h c) (s t) -> p h s c t", p=NPAIR, h=2, s=C)
            for p in range(NPAIR):
                for i_h, h in enumerate(heads):
                    inv_here = Q.dma(c_u, inv[h, p, :, :], r_view[p, i_h], r_out)
        fence()

        s_now = [sb(ctx, "s_now", [P, NPAIR, C]) for _ in range(2)]
        s_dec = sb(ctx, "s_dec", [P, NPAIR, C])
        xs = sb(ctx, "xs", [P, NPAIR, C])
        us = sb(ctx, "us", [P, NPAIR, C])
        m_s = V.do(lambda e: e.memset(s_now[0][:], 0.0))
        y_view = y_wkv[:].rearrange("p n (c t) -> p n c t", t=C)
        m_y_pe = None

        def every_head(ps, operands, *marks):
            m = None
            for p in range(NPAIR):
                for h in heads:
                    ops = operands(p, h)
                    for j, (w, x) in enumerate(ops):
                        m = mm(ps[h, p * C:(p + 1) * C], w, x, j == 0, j == len(ops) - 1, *marks,
                               signal=(p == NPAIR - 1 and h is heads[1] and j == len(ops) - 1))
            return m

        for c in range(NC):
            now, nxt = s_now[c % 2], s_now[1 - c % 2]
            blk = lambda v: v.rearrange("p (n t) -> p n t", n=NPAIR)
            n, ps, free = banks.take()
            m = every_head(ps, lambda p, h: [(ar[h, p, c, 0, :], now[h, p, :])], m_s, free)
            m_x = tt(V, xs[:], blk(ps[:, 0:256]), x_own[:, :, c, :], ALU.add, m)
            banks.release(n, m_x)
            decay = chunk_decay[:, :, c].unsqueeze(2).to_broadcast([P, NPAIR, C])
            tt(G, s_dec[:], now[:], decay, ALU.mult, m_s)
            m_dec = tt(G, s_dec[:], s_dec[:], s_own[:, :, c, :], ALU.add)
            n, ps, free = banks.take()
            m = every_head(ps, lambda p, h: [(inv[h, p, c, :], xs[h, p, :])], m_x, free)
            m_u = copy(V, us[:], blk(ps[:, 0:256]), m, m_y_pe)
            banks.release(n, m_u)
            n, ps, free = banks.take()
            m = every_head(ps, lambda p, h: [(b_hat[h, p, c, :], us[h, p, :])], m_u, free)
            m_s = tt(V, nxt[:], blk(ps[:, 0:256]), s_dec[:], ALU.add, m, m_dec, m_y_pe)
            banks.release(n, m_s)
            n, ps, free = banks.take()
            m_y_pe = every_head(ps, lambda p, h: [(now[h, p, :], ar[h, p, c, 1, :]),
                                                  (us[h, p, :], score_rb[h, p, c, :])], free)
            m = tt(V, y_view[:, :, c, :], y_view[:, :, c, :], blk(ps[:, 0:256]), ALU.add, m_y_pe)
            banks.release(n, m)
    fence()

    mixb_dram = dram("mixb_scratch", [D, L])
    with ExitStack() as ctx:
        weights = Weights(ctx, [wblock(a["w_o_rwkv_2"][0], 0, 4, i * 512, 512) for i in range(2)])
        hi = sb(ctx, "yr_hi", [P, 4, L], F32R)
        lo = sb(ctx, "yr_lo", [P, 4, L], F32R)
        gb = sb(ctx, "gb", [P, 4, L])
        bonus = sb(ctx, "bonus", [P, 4, L])
        sq, rstd = sb(ctx, "sq", [P, L]), sb(ctx, "rstd", [P, L])
        c_g = count("gate_bonus_in")
        Q.dma(c_g, gb[:], g_dram.rearrange("(k p) t -> p k t", p=P))
        here = Q.dma(c_g, bonus[:], bonus_dram.rearrange("(k p) t -> p k t", p=P))
        m_last = None
        for k in range(4):
            y = y_wkv[:, k, :]
            for half in range(2):
                n, ps, free = banks.take()
                m = mm(ps[:], headones[:], y[:, hs(half)], True, True, free)
                m1 = stt(y[:, hs(half)], ps[:], -1.0 / 64, y[:, hs(half)], ALU.mult, ALU.add, m)
                banks.release(n, m1)
            m = act(sq[:], y, ACT.Square, m1, m_last)
            for half in range(2):
                n, ps, free = banks.take()
                m1 = mm(ps[:], headones[:], sq[:, hs(half)], True, True, m, free)
                m2 = act(rstd[:, hs(half)], ps[:], ACT.Sqrt, m1, m_last, bias=gn_eps_col, scale=1.0 / 64)
                banks.release(n, m2)
            V.do(lambda e: e.reciprocal(rstd[:], rstd[:]), m2)
            tt(V, y, y, rstd[:], ALU.mult)
            m_last = ts(V, y, y, vec["ln_x_w_2"][:, k:k + 1], vec["ln_x_b_2"][:, k:k + 1], ALU.mult, ALU.add)
            m = tt(G, y, y, bonus[:, k, :], ALU.add, m_last, here)
            m = tt(G, y, y, gb[:, k, :], ALU.mult)
            m1 = act(hi[:, k, :], y, ACT.Copy, m)
            m_parts = tt(G, lo[:, k, :], y, hi[:, k, :], ALU.subtract, m1)
        gin = Ring([sb(ctx, "gate_in", [P, HALF]) for _ in range(4)], [count(f"gb_in{i}") for i in range(4)])
        store = Ring([sb(ctx, "mix_out", [P, HALF]) for _ in range(4)], [count(f"mb_out{i}") for i in range(4)])

        def to_mix_b(i, half, ps, m):
            s_, g, free = gin.take()
            g_here = Q.dma(gin.counts[s_], g[:], z_tile(Z_GATE + D + i * P, half), free)
            o_, t, free = store.take()
            m = tt(V, t[:], ps[:], g[:], ALU.mult, m, g_here, free)
            gin.release(s_, m)
            store.release(o_, Q.dma(store.counts[o_], mixb_dram[i * P:(i + 1) * P, hs(half)], t[:], m))
            return [m]

        for b in range(2):
            linear(weights, (hi, lo), 4, [(i * P, 4 * b + i) for i in range(4)], to_mix_b, [m_parts, m1])
    yw.close()
    fence()
    oc = ExitStack()
    oT = sb(oc, "oT", [P, 4, L])
    scale_qk = QH ** -0.5
    with ExitStack() as ctx:
        qT = sb(ctx, "qT", [P, NH, L])
        kT = sb(ctx, "kT", [P, NH, L])
        v_tok = sb(ctx, "v_tok", [P, SJ, 512])
        with ExitStack() as tctx:
            plan = []
            wuq, wukv = a["w_uq_2"][0], a["w_ukv_2"][0]
            w3 = lambda w, c0, n: w[:, c0:c0 + n].rearrange("(k p) c -> p k c", p=P)
            for b in range(2):
                pieces = []
                for i in range(4):
                    c0 = (4 * b + i) * QH
                    pieces += [(i * P, w3(wuq, c0, QH)), (i * P + QH, w3(wuq, c0 + QN + 16, 16)),
                               (i * P + QH + 16, w3(wuq, c0 + QN, 16))]
                plan.append((3, 512, pieces))
            plan.append(wblock(wukv, 0, 2, 0, 1024))
            weights = Weights(tctx, plan, raw=2, parts=1)
            c_hi = sb(tctx, "c_hi", [P, 3, L], F32R)
            c_lo = sb(tctx, "c_lo", [P, 3, L], F32R)
            cin = sb(tctx, "cin", [P, 3, L])
            rs_c = sb(tctx, "rs_c", [P, L])
            cos_t, sin_t = sb(tctx, "cos_t", [P, L]), sb(tctx, "sin_t", [P, L])
            c_m = [count(f"mla_in{i}") for i in range(4)]
            with ExitStack() as rctx:
                pos = sb(rctx, "pos", [P, L], I32)
                ang, t1, t2 = (sb(rctx, n_, [P, L]) for n_ in ("ang", "t1", "t2"))
                here = Q.dma(c_m[0], pos[:], a["positions_2"].to_broadcast([P, L]))
                copy(V, ang[:], pos[:], here)
                ts(V, ang[:], ang[:], inv_freq, None, ALU.mult, None)
                m = sincos(sin_t[:], cos_t[:], ang[:], (t1[:], t2[:]))
                ts(V, sin_t[:], sin_t[:], rope_sign, None, ALU.mult, None, *m)
                m_rope = (V.done, V.done.value)
            for s_ in (S, G, T, Q):
                s_.wait(m_rope)
            kpe = sb(tctx, "kpe", [P, L])
            here = Q.dma(c_m[1], kpe[:], z_tile(Z_KPE))
            tt(V, kpe[96:128, :], kpe[96:128, :], sin_t[96:128, :], ALU.mult, here)
            tt(V, kpe[64:96, :], kpe[64:96, :], cos_t[64:96, :], ALU.mult)
            copy(V, kpe[0:32, :], kpe[96:128, :])
            copy(V, kpe[32:64, :], kpe[64:96, :])
            m = tt(V, kT[64:96, 0, :], kpe[0:32, :], kpe[32:64, :], ALU.add)
            for h in range(1, NH):
                m_kpe = copy(G, kT[64:96, h, :], kT[64:96, 0, :], m)

            def latent(kt, row, g, n_ch, cnt, *marks):
                here = Q.dma(cnt, cin[:, 0:kt, :], z_dram[row:row + kt * P, :].rearrange("(k p) t -> p k t", p=P),
                             *marks)
                with ExitStack() as nctx:
                    ready = norm(nctx, cin, kt, rs_c, n_ch, here, *marks)
                for k in range(kt):
                    m = stt(cin[:, k, :], cin[:, k, :], g[:, k:k + 1], rs_c[:], ALU.mult, ALU.mult, ready)
                    m1 = act(c_hi[:, k, :], cin[:, k, :], ACT.Copy, m, *marks)
                    m = tt(V, c_lo[:, k, :], cin[:, k, :], c_hi[:, k, :], ALU.subtract, m1, *marks)
                return m

            m_lat = latent(3, 0, vec["g_q_a_2"], QLORA, c_m[2])

            def to_q(h, half, ps, m):
                q = qT[:, h, hs(half)]
                m = copy(S, q, ps[:], m)
                m1 = tt(V, q[96:128], q[96:128], sin_t[96:128, hs(half)], ALU.mult, m)
                m2 = tt(V, q[64:96], q[64:96], cos_t[64:96, hs(half)], ALU.mult)
                copy(V, rot[64:96, :], q[96:128])
                tt(V, q[64:96], q[64:96], rot[64:96, :], ALU.add)
                return [m]

            rot = sb(tctx, "rot", [P, HALF])
            for b in range(2):
                linear(weights, (c_hi, c_lo), 3, [(i * P, 4 * b + i) for i in range(4)], to_q, m_lat)
            read = [(T.done, T.done.value), (V.done, V.done.value)]
            m_lat = latent(2, QLORA, vec["g_kv_a_2"], KVLORA, c_m[3], *read)
            whi, wlo, there = weights.take()
            w, x = (whi, wlo), (c_hi, c_lo)
            for h in range(NH):
                for half in range(2):
                    n, ps, free = banks.take()
                    m = product(ps[:], three(w, x, 2, slice(h * P, (h + 1) * P), hs(half)), free, there, m_lat)
                    m = copy(evac_engine(half), kT[0:64, h, hs(half)], ps[0:64, :], m)
                    banks.release(n, m)
            for t in range(SJ):
                n, ps, free = banks.take()
                tok_ = slice(t * P, (t + 1) * P)
                pairs = []
                for k in range(2):
                    wv = [part[:, k, :].rearrange("p (h c) -> p h c", h=NH)[:, :, QN:P] for part in w]
                    pairs += [(x[0][:, k, tok_], wv[0]), (x[0][:, k, tok_], wv[1]), (x[1][:, k, tok_], wv[0])]
                m = product(ps[:].rearrange("p (h c) -> p h c", h=NH), pairs, free)
                m = copy(evac_engine(t), v_tok[:, t, :], ps[:], m)
                banks.release(n, m)
            weights.done(m)
        fence()

        with ExitStack() as tctx:
            causal = sb(tctx, "causal", [P, P])
            c_c = count("causal_in")
            c_here = Q.dma(c_c, causal[:], a["k_causal"])
            prob = [sb(tctx, "prob", [P, L]) for _ in range(2)]
            probT = [sb(tctx, "probT", [P, SJ, P]) for _ in range(2)]
            stat = [sb(tctx, "stat", [P, 8]) for _ in range(2)]
            units = [(h, i) for h in range(NH) for i in range(SJ)]
            prob_ready, probT_ready = {}, {}
            prob_read, probT_read = [None, None], [None, None]

            def softmax(n):
                h, i = units[n]
                b = n % 2
                keys = (i + 1) * P
                st = stat[b]
                pieces = [(k0, min(HALF, keys - k0)) for k0 in range(0, keys, HALF)]
                taken = []
                for k0, w in pieces:
                    nb, ps, free = banks.take()
                    m = mm(ps[:, 0:w], qT[0:QH, h, i * P:(i + 1) * P], kT[0:QH, h, k0:k0 + w], True, True, free)
                    taken.append((nb, ps, m))
                d0 = i * P - pieces[-1][0]
                ps = taken[-1][1]
                m_mask = tt(V, ps[:, d0:d0 + P], ps[:, d0:d0 + P], causal[:], ALU.add, taken[-1][2], c_here,
                            prob_ready.get(n - 2))
                for q, ((k0, w), (nb, ps, m)) in enumerate(zip(pieces, taken)):
                    V.do(lambda e, q=q, w=w, ps=ps: e.tensor_reduce(st[:, q:q + 1], ps[:, 0:w], AX.X, ALU.max),
                         m, m_mask)
                if len(pieces) == 2:
                    tt(V, st[:, 0:1], st[:, 0:1], st[:, 1:2], ALU.max)
                m_max = ts(V, st[:, 2:3], st[:, 0:1], -scale_qk, None, ALU.mult, None)
                for q, ((k0, w), (nb, ps, m)) in enumerate(zip(pieces, taken)):
                    m_e = act(prob[b][:, k0:k0 + w], ps[:, 0:w], ACT.Exp, m_max, prob_read[b],
                              bias=st[:, 2:3], scale=scale_qk, accum_out=st[:, 3 + q:4 + q])
                    banks.release(nb, m_e)
                if len(pieces) == 2:
                    tt(V, st[:, 3:4], st[:, 3:4], st[:, 4:5], ALU.add, m_e)
                V.do(lambda e: e.reciprocal(st[:, 5:6], st[:, 3:4]), m_e)
                prob_ready[n] = ts(V, prob[b][:, 0:keys], prob[b][:, 0:keys], st[:, 5:6], None, ALU.mult, None)

            def turn_prob(n):
                h, i = units[n]
                b = n % 2
                for k0 in range(0, i + 1, 4):
                    kn = min(4, i + 1 - k0)
                    nb, ps, free = banks.take()
                    for k in range(kn):
                        m = transpose(ps[:, k * P:(k + 1) * P], prob[b][:, (k0 + k) * P:(k0 + k + 1) * P],
                                      prob_ready[n], free)
                    prob_read[b] = m
                    m = copy(S if k0 else V, probT[b][:, k0:k0 + kn, :],
                             ps[:, 0:kn * P].rearrange("p (k q) -> p k q", k=kn), m, probT_read[b])
                    banks.release(nb, m)
                    probT_ready.setdefault(n, []).append(m)

            def weigh_v(n):
                h, i = units[n]
                b, rows_ = n % 2, slice(h % 2 * 64, h % 2 * 64 + 64)
                nb, ps, free = banks.take()
                for k in range(i + 1):
                    m = mm(ps[rows_, 0:P], v_tok[:, k, h * VD:(h + 1) * VD], probT[b][:, k, :], k == 0, k == i,
                           probT_ready[n], free)
                probT_read[b] = m
                m = copy(S, oT[rows_, h // 2, i * P:(i + 1) * P], ps[rows_, 0:P], m)
                banks.release(nb, m)

            for n in range(len(units) + 2):
                if n < len(units):
                    softmax(n)
                if 1 <= n <= len(units):
                    turn_prob(n - 1)
                if n >= 2:
                    weigh_v(n - 2)
        fence()

    xc = ExitStack()
    with ExitStack() as mctx:
        mix_hi = sb(mctx, "mix_hi", [P, KD, L], F32R)
        mix_lo = sb(mctx, "mix_lo", [P, KD, L], F32R)
        with ExitStack() as ctx:
            weights = Weights(ctx, [wblock(a["w_o_mla_2"][0], 0, 4, i * 512, 512) for i in range(2)])
            hi = sb(ctx, "o_hi", [P, 4, L], F32R)
            lo = sb(ctx, "o_lo", [P, 4, L], F32R)
            gin = Ring([sb(ctx, "ga_in", [P, 2, HALF]) for _ in range(2)], [count(f"ga_in{i}") for i in range(2)])
            m_ = None
            for k in range(4):
                m_ = act(hi[:, k, :], oT[:, k, :], ACT.Copy)
                m_parts = tt(V, lo[:, k, :], oT[:, k, :], hi[:, k, :], ALU.subtract, m_)

            def to_mix(i, half, ps, m):
                s_, g, free = gin.take()
                Q.dma(gin.counts[s_], g[:, 0, :], z_tile(Z_GATE + i * P, half), free)
                here = Q.dma(gin.counts[s_], g[:, 1, :], mixb_dram[i * P:(i + 1) * P, hs(half)])
                m = tt(V, g[:, 0, :], ps[:], g[:, 0, :], ALU.mult, m, here)
                m1 = tt(V, g[:, 0, :], g[:, 0, :], g[:, 1, :], ALU.add)
                m2 = act(mix_hi[:, i, hs(half)], g[:, 0, :], ACT.Copy, m1)
                m3 = tt(G, mix_lo[:, i, hs(half)], g[:, 0, :], mix_hi[:, i, hs(half)], ALU.subtract, m2)
                gin.release(s_, m2, m3)
                return [m]

            for b in range(2):
                linear(weights, (hi, lo), 4, [(i * P, 4 * b + i) for i in range(4)], to_mix, m_parts)
        fence()
        with ExitStack() as ctx:
            weights = Weights(ctx, [wblock(w_out2, 0, KD, 256 * i, 256) for i in range(4)])
            back = sb(ctx, "x_back", [P, KD, L])
            x_here = Q.dma(count("x_back"), back[:], x_dram.rearrange("(k p) t -> p k t", p=P))

            def to_x(i, half, ps, m):
                return [tt(V, back[:, i, hs(half)], back[:, i, hs(half)], ps[:], ALU.add, m, x_here)]

            for b in range(4):
                linear(weights, (mix_hi, mix_lo), KD, [(0, 2 * b), (P, 2 * b + 1)], to_x, None)
            x3_out = Q.dma(count("x3_out"), x_dram.rearrange("(k p) t -> p k t", p=P), back[:],
                           (V.done, V.done.value))
        fence()
    oc.close()
    fence()
    hT = sb(xc, "hT2", [P, KD, L])
    x_here = Q.dma(count("x_again"), hT[:], x_dram.rearrange("(k p) t -> p k t", p=P))
    with ExitStack() as ctx:
        norm(ctx, hT, KD, rs, D, x_here)
    fence()
    w_up2, w_down2 = a["w_ffn_up_2"][0], a["w_ffn_down_2"][0]
    with ExitStack() as ctx:
        plan = []
        for t0, nt in ffn_chunks(DFF2):
            plan += [wblock(w_up2, 0, KD, (t0 + q) * P, 256) for q in range(0, nt, 2)]
            plan += [wblock(w_down2, t0 * P, nt, i * 512, 512) for i in range(2)]
        weights = Weights(ctx, plan)
        hi = sb(ctx, "h2_hi", [P, KD, L], F32R)
        lo = sb(ctx, "h2_lo", [P, KD, L], F32R)
        f_hi = sb(ctx, "f2_hi", [P, FC, L], F32R)
        f_lo = sb(ctx, "f2_lo", [P, FC, L], F32R)
        f_tmp = sb(ctx, "f2_tmp", [P, 2, HALF])
        f_free = [None, None]
        ready = split_scaled(hT, vec["g_ffn_2"], hi, lo)
        f_read, marks = None, []

        def to_squared(i, half, ps, m):
            t = f_tmp[:, half, :]
            m = tt(V, t, ps[:], rs[:, hs(half)], ALU.mult, m, f_free[half])
            m1 = stt(t, t, 0.0, t, ALU.max, ALU.mult)
            f_free[half] = list(split_to(f_hi, f_lo, t, i, half, m1, f_read))
            marks.extend(f_free[half])
            return [m]

        for t0, nt in ffn_chunks(DFF2):
            marks = []
            for q in range(0, nt, 2):
                linear(weights, (hi, lo), KD, [(0, q), (P, q + 1)], to_squared, ready)
            f_read = down(weights, (f_hi, f_lo), nt, marks)
    fence()

    with ExitStack() as ctx:
        proj = sb(ctx, "proj", [P, KD, L])
        with ExitStack() as tctx:
            weights = Weights(tctx, [wblock(a["w_ple_proj_2"][0], 0, 2, 0, 1024)], raw=1, parts=1)
            p_tok = sb(tctx, "p_tok", [P, SJ, 256])
            pT = [sb(tctx, "pT", [P, 2, L], F32R) for _ in range(2)]
            here = Q.dma(count("p_in"), p_tok[:], a["p_2"][0, 0].rearrange("(t p) d -> p t d", p=P))
            for k in range(2):
                for q in range(2):
                    n, ps, free = banks.take()
                    for i in range(4):
                        m = transpose(ps[:, i * P:(i + 1) * P], p_tok[:, q * 4 + i, k * P:(k + 1) * P], here, free)
                    m1 = act(pT[0][:, k, hs(q)], ps[:], ACT.Copy, m)
                    m_p = tt(V, pT[1][:, k, hs(q)], ps[:], pT[0][:, k, hs(q)], ALU.subtract, m1)
                    banks.release(n, m1, m_p)

            def to_proj(i, half, ps, m):
                return [copy(evac_engine(half), proj[:, i, hs(half)], ps[:], m)]

            linear(weights, pT, 2, [(i * P, i) for i in range(KD)], to_proj, m_p)
            norm(tctx, hT, KD, rs, D)
        fence()
        with ExitStack() as tctx:
            weights = Weights(tctx, [wblock(a["w_ple_gate_2"][0], 0, KD, 256 * i, 256) for i in range(4)])
            hi = sb(tctx, "hp_hi", [P, KD, L], F32R)
            lo = sb(tctx, "hp_lo", [P, KD, L], F32R)
            ready = split_scaled(hT, vec["g_ple_2"], hi, lo)
            tmps = Ring([sb(tctx, "ple_tmp", [P, HALF]) for _ in range(2)])

            def to_ple(i, half, ps, m):
                s_, t, free = tmps.take()
                m = tt(V, t[:], ps[:], rs[:, hs(half)], ALU.mult, m, free)
                m1 = act(t[:], t[:], ACT.Sigmoid, m)
                m2 = tt(G, t[:], t[:], proj[:, i, hs(half)], ALU.mult, m1)
                m3 = tt(G, hT[:, i, hs(half)], hT[:, i, hs(half)], t[:], ALU.add, m2, ready)
                tmps.release(s_, m3)
                return [m]

            for b in range(4):
                linear(weights, (hi, lo), KD, [(0, 2 * b), (P, 2 * b + 1)], to_ple, ready)
        fence()

    with ExitStack() as ctx:
        ready = norm(ctx, hT, KD, rs, D)
        out_view = out[0].rearrange("(t p) d -> t p d", p=P)
        done = []
        for k in range(KD):
            done.append(stt(hT[:, k, :], hT[:, k, :], vec["g_final_2"][:, k:k + 1], rs[:], ALU.mult, ALU.mult,
                            ready))
        rows_out = [sb(ctx, "rows_out", [P, D]) for _ in range(2)]
        c_out = [count(f"out{i}") for i in range(2)]
        sent = [None, None]
        for t in range(SJ):
            b = t % 2
            parts = []
            for q in range(2):
                n, ps, free = banks.take()
                for i in range(4):
                    m = transpose(ps[:, i * P:(i + 1) * P], hT[:, q * 4 + i, t * P:(t + 1) * P],
                                  done[q * 4 + i], free)
                m = copy(evac_engine(q), rows_out[b][:, q * HALF:(q + 1) * HALF], ps[:], m, sent[b])
                banks.release(n, m)
                parts.append(m)
            sent[b] = Q.dma(c_out[b], out_view[t], rows_out[b][:], parts)
    xc.close()
    finish()
    main.close()


def constants():
    p = np.arange(P)
    f = np.float32
    vec_ = np.zeros((P, 16), f)
    vec_[:, 0] = EPS
    vec_[:, 1] = GN_EPS
    vec_[:, 2] = np.where(p < 64, 1, -1)
    vec_[:, 3] = np.where(p < 64, -1, 1)
    vec_[:, 4] = -1
    half = QR // 2
    vec_[:, 5] = (f(10000.0) ** (-np.arange(half, dtype=f) / f(half)))[p % half]
    vec_[:, 6] = np.where(p % QR < half, -1, 1)
    s, t = p[:, None] % C, np.arange(C)[None, :]
    key = np.arange(P)
    pool = np.stack([1.0 / np.minimum(np.arange(1, 17), w) for w in WINDOWS])
    return {
        "k_ident": np.eye(P, dtype=f),
        "k_ones": np.ones((P, P), f),
        "k_headones": (p[:, None] // 64 == p[None, :] // 64).astype(f),
        "k_swap": np.roll(np.eye(P, dtype=f), 64, axis=0),
        "k_vec": vec_,
        "k_wkv_mask": np.stack([t > s, t >= s], 1).astype(f).reshape(P, 2 * C),
        "k_chunk_mask": np.tile((np.arange(L) % C != 0).astype(f), (P, 1)),
        "k_causal": np.where(key[None, :] <= p[:, None], 0, -1e30).astype(f),
        "k_pool": np.tile(pool.astype(f).reshape(1, -1), (P, 1)),
    }


def kernel(**inputs):
    import concourse.bacc as bacc
    from concourse.bass_utils import run_bass_kernel_spmd

    nc = bacc.Bacc("TRN2", target_bir_lowering=False, num_devices=1)
    arrays = {n: np.ascontiguousarray(v) for n, v in inputs.items()} | constants()
    aps = {n: nc.dram_tensor("in_" + n, v.shape, mybir.dt.from_np(v.dtype), kind="ExternalInput").ap()
           for n, v in arrays.items()}
    out = nc.dram_tensor("out", (1, L, D), F32, kind="ExternalOutput").ap()
    build(nc, aps, out)
    result = run_bass_kernel_spmd(nc, [{"in_" + n: v for n, v in arrays.items()}], core_ids=[0])
    return result.results[0]["out"]
```

```python
import math
from contextlib import ExitStack

import numpy as np
import concourse.bass as bass
from concourse import mybir

F32 = mybir.dt.float32
F32R = mybir.dt.float32r
I32 = mybir.dt.int32
ALU = mybir.AluOpType
ACT = mybir.ActivationFunctionType
AX = mybir.AxisListType

P = 128
L = 1024
D = 1024
KD = D // P
HALF = 512
DFF = 2816
DFF2 = 4096
EPS = 1e-6
WINDOWS = (2, 4, 8, 16)
SG, SH, SP_ = 32, 16, 64
SJ = 8
SC = L // SJ
GB = 8
NH, QN, QR, VD = 8, 64, 32, 64
QH = QN + QR
QLORA, KVLORA = 384, 256
C = 64
HC = C // 2
NC = L // C
NPAIR = 4
GN_EPS = 64 * 1e-5
DECAY = math.exp(-0.5)
MLA_COLS = QLORA + KVLORA + QR
RWKV_COLS = 3 * 512 + 64 + 64 + 128
TWO_PI = 2 * math.pi
MAGIC = 1.5 * 2.0 ** 23


class Count:

    def __init__(self, sem):
        self.sem, self.value = sem, 0

    def add(self, n):
        self.value += n
        return (self, self.value)


class Stream:

    def __init__(self, count, chained):
        self.done, self.chained = count, chained
        self.steps, self.seen = [], {}

    def wait(self, *marks):
        for mark in marks:
            if mark is None:
                continue
            if isinstance(mark, list):
                self.wait(*mark)
                continue
            count, value = mark
            if value > self.seen.get(id(count), 0):
                self.seen[id(count)] = value
                self.steps.append(("wait", count.sem, value))

    def do(self, make, *marks, signal=True):
        self.wait(*marks)
        if self.chained and self.done.value:
            self.wait((self.done, self.done.value))
        if not signal:
            self.steps.append(("do", make, None, 0))
            return None
        self.steps.append(("do", make, self.done.sem, 1))
        return self.done.add(1)

    def dma(self, count, out, in_, *marks):
        self.wait(*marks)
        self.steps.append(("do", lambda e: e.dma_start(out, in_), count.sem, 16))
        return count.add(16)

    def play(self, engine):
        for kind, what, *rest in self.steps:
            if kind == "wait":
                engine.wait_ge(what, rest[0])
            else:
                ins = what(engine)
                if rest[0] is not None:
                    ins.then_inc(rest[0], rest[1])


class Ring:

    def __init__(self, tiles, counts=None):
        self.tiles, self.counts = tiles, counts
        self.free = [[] for _ in tiles]
        self.at = -1

    def take(self):
        self.at = (self.at + 1) % len(self.tiles)
        return self.at, self.tiles[self.at], self.free[self.at]

    def release(self, n, *marks):
        self.free[n] = list(marks)


def build(nc, a, out):
    main = ExitStack()
    counts = []

    def count(name):
        c = Count(main.enter_context(nc.semaphore(name)))
        counts.append(c)
        return c

    V = Stream(count("vector_done"), True)
    S = Stream(count("scalar_done"), True)
    G = Stream(count("gpsimd_done"), True)
    T = Stream(count("tensor_done"), False)
    Q = Stream(count("sync_done"), False)
    streams = [V, S, G, T, Q]

    def finish():
        Q.wait(*[(c, c.value) for c in counts if c is not Q.done])
        with nc.Block() as block:
            for stream, on in ((V, block.vector), (S, block.scalar), (G, block.gpsimd), (T, block.tensor),
                               (Q, block.sync)):
                on(stream.play)

    names = [0]

    def sb(ctx, name, shape, dt=F32, side="left"):
        names[0] += 1
        return ctx.enter_context(nc.sbuf_tensor(f"{name}_{names[0]}", shape, dt, side=side))

    def now():
        return [(c, c.value) for c in counts]

    def fence(*without):
        for s in streams:
            if s in without:
                continue
            s.wait(*[(c, c.value) for c in counts if c is not s.done or s.chained])

    banks = Ring([main.enter_context(nc.psum_tensor(f"bank{i}", [P, HALF], F32)) for i in range(8)])

    def dram(name, shape):
        return nc.dram_tensor(name, shape, F32).ap()

    z_dram = dram("z_scratch", [36 * P, L])
    x_dram = dram("x_scratch", [D, L])
    n_dram = dram("n_scratch", [P, 2 * HC * HC])
    r_dram = dram("r_scratch", [P, 2 * HC * HC])
    rt_dram = dram("r_turned_scratch", [P, HC * HC])
    g_dram = dram("gate_scratch", [512, L])
    bonus_dram = dram("bonus_scratch", [512, L])
    proj_dram = dram("proj_scratch", [D, L])

    c_const = count("consts_in")
    const = {}

    def load_const(name, ap, shape, dt=F32):
        t = sb(main, name, shape, dt)
        Q.dma(c_const, t[:], ap)
        const[name] = t
        return t

    ident = load_const("ident", a["k_ident"], [P, P])
    headones = load_const("headones", a["k_headones"], [P, P])
    ones = load_const("ones", a["k_ones"], [P, P])
    kvec = load_const("kvec", a["k_vec"], [P, 16])
    channel_vectors = (("norm_mix", D), ("norm_ffn", D), ("pool_scale", 512), ("b_glu", 512),
                       ("norm_final", D), ("g_mix_2", D), ("g_q_a_2", QLORA), ("g_kv_a_2", KVLORA),
                       ("mu_rwkv_2", RWKV_COLS), ("w0_2", 512), ("a0_2", 512), ("k_k_2", 512), ("k_a_2", 512),
                       ("r_k_2", 512), ("ln_x_w_2", 512), ("ln_x_b_2", 512), ("g_ffn_2", D), ("g_ple_2", D),
                       ("g_final_2", D))
    vec_rows = sb(main, "vec_rows", [P, P])
    vec_cols = sb(main, "vec_cols", [P, P])
    vec, row = {}, 0
    for name, n in channel_vectors:
        v = a[name] if len(a[name].shape) == 1 else a[name][0]
        v = v.rearrange("h n -> (h n)") if len(v.shape) == 2 else v
        Q.dma(c_const, vec_rows[row:row + n // P, :], v.rearrange("(k p) -> k p", p=P))
        vec[name] = vec_cols[:, row:row + n // P]
        row += n // P
    n_vec = row
    consts_in = (c_const, c_const.value)
    eps_col, gn_eps_col, sign_pm, sign_mp, minus_one, inv_freq, rope_sign = (
        kvec[:, i:i + 1] for i in range(7))
    for s in (V, S, G, T):
        s.wait(consts_in)

    n, ps, free = banks.take()
    m = T.do(lambda e, ps=ps: e.transpose(ps[:, 0:n_vec], vec_rows[0:n_vec, :], ident[0:n_vec, 0:n_vec]))
    m = V.do(lambda e, ps=ps: e.tensor_copy(vec_cols[:, 0:n_vec], ps[:, 0:n_vec]), m)
    banks.release(n, m)
    for s in (S, G):
        s.wait(m)

    rs = sb(main, "rs", [P, L])
    rs_ready = [None]

    def evac_engine(n):
        return V if n % 2 == 0 else S

    def copy(eng, o, i, *marks):
        if eng is S:
            return S.do(lambda e: e.activation(o, i, ACT.Copy), *marks)
        return eng.do(lambda e: e.tensor_copy(o, i), *marks)

    def tt(eng, o, x, y, op, *marks):
        return eng.do(lambda e: e.tensor_tensor(o, x, y, op), *marks)

    def ts(eng, o, x, s1, s2, op0, op1, *marks):
        if s2 is None:
            return eng.do(lambda e: e.tensor_scalar(o, x, s1, None, op0), *marks)
        return eng.do(lambda e: e.tensor_scalar(o, x, s1, s2, op0, op1), *marks)

    def stt(o, x, s1, y, op0, op1, *marks):
        return V.do(lambda e: e.scalar_tensor_tensor(out=o, in0=x, scalar=s1, in1=y, op0=op0, op1=op1),
                    *marks)

    def act(o, x, f, *marks, **kw):
        return S.do(lambda e: e.activation(o, x, f, **kw), *marks)

    def mm(o, w, x, start, stop, *marks, signal=None):
        return T.do(lambda e: e.matmul(o, w, x, start=start, stop=stop), *marks,
                    signal=stop if signal is None else signal)

    def transpose(o, i, *marks):
        return T.do(lambda e: e.transpose(o, i, ident[0:i.shape[0], 0:i.shape[0]]), *marks)

    class Weights:

        SIZE = 2048

        def __init__(self, ctx, plan, raw=3, parts=2, side="left"):
            self.RAW, self.PARTS = raw, parts
            self.raw = Ring([sb(ctx, "w_raw", [P, self.SIZE], side=side) for _ in range(self.RAW)],
                            [count(f"w_in_{names[0]}_{i}") for i in range(self.RAW)])
            self.hi = [sb(ctx, "w_hi", [P, self.SIZE], F32R, side) for _ in range(self.PARTS)]
            self.lo = [sb(ctx, "w_lo", [P, self.SIZE], F32R, side) for _ in range(self.PARTS)]
            self.used = [[] for _ in range(self.PARTS)]
            self.plan, self.loaded, self.split, self.next = plan, {}, {}, 0
            for i in range(min(self.RAW, len(plan))):
                self.load(i)

        def load(self, i):
            kt, cols, pieces = self.plan[i]
            n, tile, free = self.raw.take()
            view = tile[:, 0:kt * cols].rearrange("p (k c) -> p k c", k=kt)
            for c0, src in pieces:
                self.loaded[i] = (n, Q.dma(self.raw.counts[n], view[:, :, c0:c0 + src.shape[2]], src, free))

        def split_block(self, i):
            kt, cols, _ = self.plan[i]
            n, here = self.loaded.pop(i)
            size = kt * cols
            raw, hi, lo = (t[:, 0:size] for t in (self.raw.tiles[n], self.hi[i % self.PARTS], self.lo[i % self.PARTS]))
            m1 = copy(S, hi, raw, here, self.used[i % self.PARTS])
            m2 = tt(V, lo, raw, hi, ALU.subtract, here, m1, self.used[i % self.PARTS])
            self.raw.release(n, m1, m2)
            view = lambda t: t.rearrange("p (k c) -> p k c", k=kt)
            self.split[i] = (view(hi), view(lo), [m1, m2])

        def take(self):
            i = self.next
            self.next += 1
            if i not in self.split:
                self.split_block(i)
            if self.PARTS > 1 and i + 1 < len(self.plan) and i + 1 not in self.split:
                self.split_block(i + 1)
            for j in range(i + self.PARTS, i + self.PARTS + self.RAW):
                if j < len(self.plan) and j not in self.loaded and j not in self.split:
                    self.load(j)
            return self.split.pop(i)

        def done(self, mark):
            self.used[(self.next - 1) % self.PARTS] = [mark]

    def wblock(w, k0, kt, c0, cols):
        return (kt, cols, [(0, w[k0:k0 + kt * P, c0:c0 + cols].rearrange("(k p) c -> p k c", p=P))])

    def product(ps, pairs, *marks):
        m = None
        for i, (w, x) in enumerate(pairs):
            m = mm(ps, w, x, i == 0, i == len(pairs) - 1, *(marks if i == 0 else ()))
        return m

    def three(w, x, kt, wc, xc):
        out_ = []
        for k in range(kt):
            out_ += [(w[0][:, k, wc], x[0][:, k, xc]), (w[0][:, k, wc], x[1][:, k, xc]),
                     (w[1][:, k, wc], x[0][:, k, xc])]
        return out_

    def grouped(w, x, kt, jobs, there, ready, evac):
        by_k = isinstance(ready, dict)
        taken = [banks.take() for _ in jobs]
        marks = [None] * len(jobs)
        for k in range(kt):
            for j, (wc, xc, _) in enumerate(jobs):
                _, ps, free = taken[j]
                pairs = [(w[0][:, k, wc], x[0][:, k, xc]), (w[0][:, k, wc], x[1][:, k, xc]),
                         (w[1][:, k, wc], x[0][:, k, xc])]
                for i, (a_, b_) in enumerate(pairs):
                    first, last = k == 0 and i == 0, k == kt - 1 and i == 2
                    wait = [free, there] if first else []
                    wait.append(ready[k] if by_k else ready)
                    marks[j] = mm(ps[:], a_, b_, first, last, *wait)
        for (n, ps, _), m, (_, _, args) in zip(taken, marks, jobs):
            banks.release(n, *evac(*args, ps, m))
        return marks[-1]

    def linear(weights, x, kt, tiles, evac, ready):
        hi, lo, there = weights.take()
        jobs = [(slice(c0, c0 + P), hs(half), (index, half)) for c0, index in tiles for half in range(2)]
        for j in range(0, len(jobs), 4):
            last = grouped((hi, lo), x, kt, jobs[j:j + 4], there, ready, evac)
        weights.done(last)
        return last

    def hs(half):
        return slice(half * HALF, half * HALF + HALF)

    def split_tile(k, src, g, hi, lo, *marks):
        m = act(hi[:, k, :], src, ACT.Copy, *marks, scale=g)
        return [m, stt(lo[:, k, :], src, g, hi[:, k, :], ALU.mult, ALU.subtract, m, *marks)]

    def split_scaled(hT, g, hi, lo, *marks):
        return {k: split_tile(k, hT[:, k, :], g[:, k:k + 1], hi, lo, *marks) for k in range(KD)}

    class Norm:

        def __init__(self, sq, acc, read):
            self.sq, self.acc, self.read, self.born, self.n = sq, acc, read, None, 0

        def add(self, x, *marks, scale=1.0, engine=None):
            if self.n == 0:
                self.m = act(self.acc[:], x, ACT.Square, self.born, *marks, scale=scale)
            else:
                sq = self.sq[self.n % 2]
                m = act(sq[:], x, ACT.Square, self.read[self.n % 2], *marks, scale=scale)
                self.m = self.read[self.n % 2] = tt(engine or G, self.acc[:], self.acc[:], sq[:], ALU.add, m,
                                                    self.m)
            self.n += 1

        def columns(self, dst):
            n, ps, free = banks.take()
            for j in range(L // P):
                m = mm(ps[:, j:j + 1], self.acc[:, j * P:(j + 1) * P], ones[:, 0:1], True, True, self.m, free)
            self.born, self.n = m, 0
            m = copy(V, dst, ps[:, 0:L // P], m)
            banks.release(n, m)
            return m

        def finish(self, dst, n_ch, *marks):
            col_ = ncol[:, 0, :]
            m = self.columns(col_)
            m = act(col_, col_, ACT.Sqrt, m, bias=eps_col, scale=1.0 / n_ch)
            m = V.do(lambda e: e.reciprocal(col_, col_), m)
            return spread(dst, col_, m, *marks)

    ncol = sb(main, "norm_cols", [P, 3, L // P])

    def spread(dst, col_, m, *marks):
        out_ = []
        for half in range(2):
            n, ps, free = banks.take()
            for i in range(4):
                j = half * 4 + i
                m1 = mm(ps[:, i * P:(i + 1) * P], col_[:, j:j + 1].to_broadcast([P, P]), ident[:], True, True,
                        m, free)
            m1 = copy(evac_engine(half), dst[:, hs(half)], ps[:], m1, *marks)
            banks.release(n, m1)
            out_.append(m1)
        return out_

    def new_norm(ctx):
        return Norm([sb(ctx, "sq", [P, L]) for _ in range(2)], sb(ctx, "sq_sum", [P, L]), [None, None])

    def norm(ctx, x, kt, dst, n, *marks):
        nm = new_norm(ctx)
        for k in range(kt):
            nm.add(x[:, k, :], *marks, engine=V)
        return nm.finish(dst, n)

    w_in, w_glu, w_out = a["w_in"][0], a["w_glu"][0], a["w_out"][0]
    w_gate, w_up, w_down = a["w_gate"][0], a["w_up"][0], a["w_down"][0]

    res = ExitStack()
    hT = sb(res, "hT", [P, KD, L])
    u_ctx = ExitStack()
    u_pool = sb(u_ctx, "u_pool", [P, 4, L])
    u_tok = sb(u_ctx, "u_tok", [P, SG, SJ, SH])
    rs_col = sb(u_ctx, "rs_col", [P, SJ])

    with ExitStack() as ctx:
        x_tok = sb(ctx, "x_tok", [P, SJ, D])
        junk = sb(ctx, "junk", [P, D])
        c_x = [count(f"x_in{i}") for i in range(2)]
        x_view = a["x"][0].rearrange("(c j) d -> c j d", j=SJ)
        hT_view = hT[:].rearrange("p k (c j) -> p k j c", j=SJ)
        for part in range(2):
            js = slice(part * 4, part * 4 + 4)
            Q.dma(c_x[part], x_tok[:, js, :], x_view[:, js, :])
        for j in range(SJ):
            x_here = (c_x[j // 4], 16)
            m = S.do(lambda e, j=j: e.activation(junk[:], x_tok[:, j, :], ACT.Square,
                                                 accum_out=rs_col[:, j:j + 1]), x_here)
        m = act(rs_col[:], rs_col[:], ACT.Sqrt, m, bias=eps_col, scale=1.0 / D)
        rs_col_ready = V.do(lambda e: e.reciprocal(rs_col[:], rs_col[:]), m)
        n_ev = 0
        for part in range(2):
            for k in range(KD):
                n, ps, free = banks.take()
                for i in range(4):
                    j = part * 4 + i
                    m = transpose(ps[:, i * P:(i + 1) * P], x_tok[:, j, k * P:(k + 1) * P],
                                  (c_x[part], 16), free)
                n_ev += 1
                m = copy(evac_engine(n_ev), hT_view[:, k, part * 4:part * 4 + 4, :],
                         ps[:].rearrange("p (j c) -> p j c", j=4), m)
                banks.release(n, m)
        rs_view = rs[:].rearrange("p (c j) -> p j c", j=SJ)
        for part in range(2):
            n, ps, free = banks.take()
            for i in range(4):
                j = part * 4 + i
                m = mm(ps[:, i * P:(i + 1) * P], rs_col[:, j:j + 1].to_broadcast([P, P]), ident[:],
                       True, True, rs_col_ready, free)
            m = copy(V, rs_view[:, part * 4:part * 4 + 4, :], ps[:].rearrange("p (j c) -> p j c", j=4), m)
            banks.release(n, m)
    fence()

    with ExitStack() as ctx:
        weights = Weights(ctx, [wblock(w_in, 0, KD, 256 * i, 256) for i in range(4)])
        hi = sb(ctx, "hg_hi", [P, KD, L], F32R)
        lo = sb(ctx, "hg_lo", [P, KD, L], F32R)
        ready = split_scaled(hT, vec["norm_mix"], hi, lo)

        def to_pool(i, half, ps, m):
            return [tt(V, u_pool[:, i, hs(half)], ps[:], rs[:, hs(half)], ALU.mult, m)]

        for b in range(2):
            linear(weights, (hi, lo), KD, [(0, 2 * b), (P, 2 * b + 1)], to_pool, ready)
        tok = [t[:].rearrange("p k (c j) -> p k j c", j=SJ) for t in (hi, lo)]
        for b in range(2):
            whi, wlo, there = weights.take()
            for j in range(SJ):
                n, ps, free = banks.take()
                pairs = []
                for k in range(KD):
                    pairs += [(tok[0][:, k, j, :], whi[:, k, :]), (tok[0][:, k, j, :], wlo[:, k, :]),
                              (tok[1][:, k, j, :], whi[:, k, :])]
                last = product(ps[:, 0:256], pairs, free, there, list(ready.values()))
                o = u_tok[:, 16 * b:16 * b + 16, j, :]
                i_ = ps[:, 0:256].rearrange("p (g h) -> p g h", h=SH)
                m = act(o, i_, ACT.Copy, last, scale=rs_col[:, j:j + 1])
                banks.release(n, m)
            weights.done(last)
    fence()

    def sincos(sin_o, cos_o, theta, tmp, *marks):
        t, r = tmp
        c1 = 6.28125
        c2 = float(np.float32((TWO_PI - c1) // 2.0 ** -20 * 2.0 ** -20))
        c3 = TWO_PI - c1 - c2
        ts(V, t, theta, 1.0 / TWO_PI, MAGIC, ALU.mult, ALU.add, *marks)
        ts(V, t, t, -MAGIC, None, ALU.add, None)
        stt(r, t, -c1, theta, ALU.mult, ALU.add)
        stt(r, t, -c2, r, ALU.mult, ALU.add)
        stt(r, t, -c3, r, ALU.mult, ALU.add)
        top = float(np.float32(3.1415925))
        m = ts(V, r, r, top, -top, ALU.min, ALU.max)
        m2 = act(sin_o, r, ACT.Sin, m)
        m3 = act(t, r, ACT.Sin, m, scale=0.5)
        m4 = tt(V, t, t, t, ALU.mult, m3)
        return ts(V, cos_o, t, -2.0, 1.0, ALU.mult, ALU.add, m4), m2

    def cmul(o, x, y, tmp, *marks):
        tt(V, tmp, x[1], y[1], ALU.mult, *marks)
        tt(V, o[0], x[0], y[0], ALU.mult)
        tt(V, o[0], o[0], tmp, ALU.subtract)
        tt(V, tmp, x[1], y[0], ALU.mult)
        tt(V, o[1], x[0], y[1], ALU.mult)
        return tt(V, o[1], o[1], tmp, ALU.add)

    y_ctx = ExitStack()
    y_tok = sb(y_ctx, "y_tok", [P, SJ, SG, SH])
    w_pool = sb(y_ctx, "w_pool", [P, 4, P])
    inv_n = sb(y_ctx, "inv_n", [P, 4, 16])
    with ExitStack() as ctx:
        sums = [sb(ctx, "window_sum", [P, L])[:] for _ in range(2)]
        c_pool = count("pool_in")
        Q.dma(c_pool, inv_n[:].rearrange("p w n -> p (w n)"), a["k_pool"])
        pool_here = Q.dma(c_pool, w_pool[:], a["w_pool"][0].rearrange("g c d -> c g d"))
        for i, w in enumerate(WINDOWS):
            src = u_pool[:, i, :]
            lag, b = 1, 0
            while lag < w:
                dst = sums[b]
                copy(G, dst[:, 0:lag], src[:, 0:lag])
                tt(G, dst[:, lag:L], src[:, lag:L], src[:, 0:L - lag], ALU.add)
                src, lag, b = dst, 2 * lag, 1 - b
            tt(G, src[:, 0:16], src[:, 0:16], inv_n[:, i, :], ALU.mult, pool_here)
            ts(G, src[:, 16:L], src[:, 16:L], 1.0 / w, None, ALU.mult, None)
            pooled = tt(G, u_pool[:, i, :], src, u_pool[:, i, :], ALU.subtract)
        c_s = count("ssm_params_in")
        lam_rows = sb(ctx, "lam_rows", [SG, 4, SP_])
        dt = sb(ctx, "dt", [P, SG])
        bx = sb(ctx, "bx", [P, SG, SH])
        by = sb(ctx, "by", [P, SG, SH])
        c_rows = sb(ctx, "c_rows", [P, 4, 2, P])
        d_row = sb(ctx, "d_row", [P, SG * SH])
        swap = sb(ctx, "swap", [P, P])
        re, im = (a[n][0] for n in ("lam_re", "lam_im"))
        b_re, b_im = (a[n][0].rearrange("g p h -> p g h") for n in ("b_re", "b_im"))
        c_re, c_im = (a[n][0].rearrange("g h p -> (g h) p").rearrange("(n r) p -> r n p", r=P)
                      for n in ("c_re", "c_im"))
        for i, w in enumerate((re, re, im, im)):
            Q.dma(c_s, lam_rows[:, i, :], w)
        Q.dma(c_s, dt[:], a["log_dt"].to_broadcast([P, SG]))
        for t, top, bottom in ((bx, b_re, b_im), (by, b_im, b_re)):
            Q.dma(c_s, t[0:64], top)
            Q.dma(c_s, t[64:128], bottom)
        for i, (left, right) in enumerate(((c_re, c_im), (c_im, c_re))):
            Q.dma(c_s, c_rows[:, :, i, 0:64], left)
            Q.dma(c_s, c_rows[:, :, i, 64:128], right)
        Q.dma(c_s, d_row[:], a["d_skip"][0].rearrange("(a g) h -> a (g h)", a=1).to_broadcast([P, SG * SH]))
        here = Q.dma(c_s, swap[:], a["k_swap"])

        n, ps, free = banks.take()
        m = transpose(ps[:, 0:SG], lam_rows[:, 0:2, :].rearrange("g a p -> g (a p)"), here, free)
        m = transpose(ps[:, SG:2 * SG], lam_rows[:, 2:4, :].rearrange("g a p -> g (a p)"), here, free)
        lam = sb(ctx, "lam", [P, 2, SG])
        m = copy(V, lam[:], ps[:, 0:2 * SG].rearrange("p (a g) -> p a g", a=2), m)
        banks.release(n, m)
        lr, li = lam[:, 0, :], lam[:, 1, :]
        small = lambda name: sb(ctx, name, [P, SG])
        mag, r8, theta, tmp1, tmp2, sn, cs = (small(n_) for n_ in
                                              ("mag", "r8", "theta", "tmp1", "tmp2", "sn", "cs"))
        m = act(dt[:], dt[:], ACT.Exp, here)
        tt(V, theta[:], li, dt[:], ALU.mult, m)
        m = tt(V, tmp1[:], lr, dt[:], ALU.mult)
        act(mag[:], tmp1[:], ACT.Exp, m)
        m = act(r8[:], tmp1[:], ACT.Exp, m, scale=float(SJ))
        m = sincos(sn[:], cs[:], theta[:], (tmp1[:], tmp2[:]), m)
        pw = sb(ctx, "pw", [P, 2, SJ + 1, SG])
        V.do(lambda e: e.memset(pw[:, 0, 0, :], 1.0))
        V.do(lambda e: e.memset(pw[:, 1, 0, :], 0.0))
        tt(V, pw[:, 0, 1, :], mag[:], cs[:], ALU.mult, *m)
        tt(V, pw[:, 1, 1, :], mag[:], sn[:], ALU.mult)
        for i in range(2, SJ + 1):
            cmul((pw[:, 0, i, :], pw[:, 1, i, :]), (pw[:, 0, i - 1, :], pw[:, 1, i - 1, :]),
                 (pw[:, 0, 1, :], pw[:, 1, 1, :]), tmp1[:])
        den, nr, cf = small("den"), small("nr"), sb(ctx, "cf", [P, 2, SG])
        tt(V, den[:], lr, lr, ALU.mult)
        tt(V, tmp1[:], li, li, ALU.mult)
        tt(V, den[:], den[:], tmp1[:], ALU.add)
        V.do(lambda e: e.reciprocal(den[:], den[:]))
        ts(V, nr[:], pw[:, 0, 1, :], -1.0, None, ALU.add, None)
        ni = pw[:, 1, 1, :]
        for i, (p_, q_, op) in enumerate((((nr[:], lr), (ni, li), ALU.add), ((ni, lr), (nr[:], li), ALU.subtract))):
            tt(V, cf[:, i, :], *p_, ALU.mult)
            tt(V, tmp1[:], *q_, ALU.mult)
            tt(V, cf[:, i, :], cf[:, i, :], tmp1[:], op)
            tt(V, cf[:, i, :], cf[:, i, :], den[:], ALU.mult)
        gains = sb(ctx, "gains", [P, 2, SG, SJ])
        for s_ in range(SJ):
            m_gains = cmul((gains[:, 0, :, s_], gains[:, 1, :, s_]),
                           (pw[:, 0, SJ - 1 - s_, :], pw[:, 1, SJ - 1 - s_, :]), (cf[:, 0, :], cf[:, 1, :]),
                           tmp1[:])
        turn = sb(ctx, "turn", [P, 2, 8, SG])
        copy(V, turn[:, 0, 0, :], cs[:])
        ts(V, turn[:, 1, 0, :], sn[:], sign_pm, None, ALU.mult, None)
        for k in range(3):
            cmul((tmp2[:], nr[:]), (turn[:, 0, 0, :], turn[:, 1, 0, :]), (turn[:, 0, 0, :], turn[:, 1, 0, :]),
                 tmp1[:])
            copy(V, turn[:, 0, 0, :], tmp2[:])
            copy(V, turn[:, 1, 0, :], nr[:])
        for k in range(1, 7):
            cmul((turn[:, 0, k, :], turn[:, 1, k, :]), (turn[:, 0, k - 1, :], turn[:, 1, k - 1, :]),
                 (turn[:, 0, k - 1, :], turn[:, 1, k - 1, :]), tmp1[:])
        ts(V, by[:], by[:], sign_mp, None, ALU.mult, None)
        cx = sb(ctx, "cx", [P, SG, SH])
        cy = sb(ctx, "cy", [P, SG, SH])
        for i, (t, sign) in enumerate(((cx, sign_pm), (cy, minus_one))):
            n, ps, free = banks.take()
            for q in range(4):
                m = transpose(ps[:, q * P:(q + 1) * P], c_rows[:, q, i, :], here, free)
            m_c = ts(V, t[:].rearrange("p g h -> p (g h)"), ps[:], sign, None, ALU.mult, None, m)
            banks.release(n, m_c)

        lead = sb(ctx, "lead", [P, GB, 2 * SJ - 1, SH])
        m_lead0 = G.do(lambda e: e.memset(lead[:], 0.0))
        tmp = sb(ctx, "tmp", [P, GB * SC])
        ca = sb(ctx, "ca", [P, GB, SJ, SH])
        state_in = [sb(ctx, "state_in", [P, GB, P]) for _ in range(2)]
        toep = sb(ctx, "toep", [P, GB, P])
        u_rows = sb(ctx, "u_rows", [P, GB, SC])
        phase = sb(ctx, "phase", [P, 2, GB, SC])
        step = sb(ctx, "step", [P, GB, SC])
        z = sb(ctx, "z", [P, GB, SC])
        state = sb(ctx, "state", [P, GB, SC + 1])
        m_zero = G.do(lambda e: e.memset(state[:], 0.0))
        du = sb(ctx, "du", [P, SJ, SG, SH])
        m_du = None
        for j in range(SJ):
            m_du = tt(G, du[:, j, :, :], u_tok[:, :, j, :],
                      d_row[:].rearrange("p (g h) -> p g h", h=SH), ALU.mult, here)
        m_state_read = m_toep_read = m_u_read = m_ca_read = None
        for b in range(SG // GB):
            gs = slice(b * GB, b * GB + GB)
            shape = [P, GB, SJ, SH]
            over_h = lambda v: v.unsqueeze(3).to_broadcast(shape)
            over_j = lambda v: v.unsqueeze(2).to_broadcast(shape)
            tview = tmp[:, 0:GB * SJ * SH].rearrange("p (g j h) -> p g j h", g=GB, j=SJ)
            pv = lambda i: pw[:, i, 1:SJ + 1, gs].rearrange("p j g -> p g j")
            tt(V, lead[:, :, 0:SJ, :], over_h(gains[:, 0, gs, :]), over_j(bx[:, gs, :]), ALU.mult,
               m_lead0, m_toep_read)
            tt(V, tview, over_h(gains[:, 1, gs, :]), over_j(by[:, gs, :]), ALU.mult)
            m_lead = tt(V, lead[:, :, 0:SJ, :], lead[:, :, 0:SJ, :], tview, ALU.add)
            tt(V, ca[:], over_h(pv(0)), over_j(cx[:, gs, :]), ALU.mult, m_ca_read)
            tt(V, tview, over_h(pv(1)), over_j(cy[:, gs, :]), ALU.mult)
            m_ca = tt(V, ca[:], ca[:], tview, ALU.add)
            for q in range(2):
                n, ps, free = banks.take()
                for i in range(4):
                    g = b * GB + q * 4 + i
                    m = transpose(ps[:, i * P:(i + 1) * P], u_tok[:, g, :, :].rearrange("p j h -> p (j h)"),
                                  free)
                m_u = copy(S, u_rows[:, q * 4:q * 4 + 4, :], ps[:].rearrange("p (g c) -> p g c", g=4), m,
                           m_u_read)
                banks.release(n, m_u)
            for q in range(2):
                n, ps, free = banks.take()
                for i in range(4):
                    m = transpose(ps[:, i * P:(i + 1) * P],
                                  lead[:, q * 4 + i, 0:SJ, :].rearrange("p s h -> p (s h)"), m_lead, free)
                v = ps[:].rearrange("p (g a q) -> p g a q", g=4, a=2)
                o = [t[:, q * 4:q * 4 + 4, :].rearrange("p g (a q) -> p g a q", a=2) for t in state_in]
                copy(V, o[0], v, m, m_state_read)
                copy(V, o[1][:, :, 0, :], v[:, :, 1, :])
                m_in = copy(V, o[1][:, :, 1, :], v[:, :, 0, :])
                banks.release(n, m_in)
            for q in range(2):
                n, ps, free = banks.take()
                for i in range(4):
                    for j in range(SJ):
                        lag = lead[:, q * 4 + i, SJ - 1 - j:2 * SJ - 1 - j, :].rearrange("p s h -> p (s h)")
                        m = mm(ps[:, i * P + j * SH:i * P + (j + 1) * SH], lag, cx[:, b * GB + q * 4 + i, :],
                               True, True, m_lead, m_c, free)
                m_toep_read = m
                m_toep = copy(S, toep[:, q * 4:q * 4 + 4, :], ps[:].rearrange("p (g n) -> p g n", g=4), m,
                              m_u_read)
                banks.release(n, m_toep)
            V.do(lambda e: e.memset(phase[:, 0, :, 0:1], 1.0))
            V.do(lambda e: e.memset(phase[:, 1, :, 0:1], 0.0))
            for k in range(7):
                w = 1 << k
                by_turn = lambda i: turn[:, i, k, gs].unsqueeze(2).to_broadcast([P, GB, w])
                cmul((phase[:, 0, :, w:2 * w], phase[:, 1, :, w:2 * w]),
                     (phase[:, 0, :, 0:w], phase[:, 1, :, 0:w]), (by_turn(0), by_turn(1)),
                     tmp[:, 0:GB * w].rearrange("p (g w) -> p g w", g=GB))
            m_phase = copy(V, step[:], r8[:, gs].unsqueeze(2).to_broadcast([P, GB, SC]))
            V.do(lambda e: e.memset(step[:, :, 0:1], 0.0))
            tm = tmp[:].rearrange("p (g c) -> p g c", g=GB)
            for q in range(2):
                qs = slice(q * 4, q * 4 + 4)
                both = []
                for s_ in range(2):
                    n, ps, free = banks.take()
                    for i in range(4):
                        m = mm(ps[:, i * P:(i + 1) * P], state_in[s_][:, q * 4 + i, :],
                               u_rows[:, q * 4 + i, :], True, True, m_in, m_u, free)
                    both.append((n, ps, m))
                m_state_read = m
                flat = lambda v: v.rearrange("p g c -> p (g c)")
                m1 = tt(V, flat(z[:, qs, :]), flat(phase[:, 0, qs, :]), both[0][1][:], ALU.mult, both[0][2])
                m2 = tt(V, flat(tm[:, qs, :]), flat(phase[:, 1, qs, :]), both[1][1][:], ALU.mult, both[1][2])
                banks.release(both[0][0], m1)
                banks.release(both[1][0], m2)
            fz, fm = flat(z[:]), flat(tm)
            tt(V, fz, fz, fm, ALU.add)
            m_z = V.do(lambda e: e.tensor_tensor_scan(fz, flat(step[:]), fz, 0.0, ALU.mult, ALU.add))
            for q in range(2):
                qs = slice(q * 4, q * 4 + 4)
                n, ps, free = banks.take()
                m = mm(ps[:], swap[:], flat(z[:, qs, :]), True, True, m_z, free)
                m1 = tt(V, flat(tm[:, qs, :]), flat(phase[:, 1, qs, :]), ps[:], ALU.mult, m)
                banks.release(n, m1)
            tt(V, fz, fz, flat(phase[:, 0, :, :]), ALU.mult)
            m_state = tt(V, state[:, :, 1:SC + 1], z[:], tm, ALU.subtract, m_ca_read, m_zero)
            for q in range(2):
                n, ps, free = banks.take()
                for i in range(4):
                    g = q * 4 + i
                    o = ps[:, i * P:(i + 1) * P]
                    mm(o, u_rows[:, g, :], toep[:, g, :], True, False, m_toep, free)
                    m = mm(o, state[:, g, 0:SC], ca[:, g, :, :].rearrange("p j h -> p (j h)"), False, True,
                           m_state, m_ca)
                m_u_read = m_ca_read = m
                m1 = V.do(lambda e, o=y_tok[:, :, b * GB + q * 4:b * GB + q * 4 + 4, :],
                          i_=ps[:].rearrange("p (g j h) -> p j g h", g=4, j=SJ): e.tensor_copy(o, i_), m)
                banks.release(n, m1)
        m = tt(V, y_tok[:].rearrange("p j g h -> p (j g h)"), y_tok[:].rearrange("p j g h -> p (j g h)"),
               du[:].rearrange("p j g h -> p (j g h)"), ALU.add, m_du)
        for j in range(SJ):
            y_j = y_tok[:, j, :, :].rearrange("p g h -> p (g h)")
            m_gelu = act(y_j, y_j, ACT.Gelu_apprx_tanh, m)
    fence()
    FC = 4

    def ffn_chunks(d_ff):
        n_t = d_ff // P
        return [(t0, min(FC, n_t - t0)) for t0 in range(0, n_t, FC)]

    w_in2, w_out2 = a["w_in_2"][0], a["w_out_2"][0]
    plan = [wblock(w_glu, 0, 4, 0, 512)] + [wblock(w_out, 0, KD, 256 * i, 256) for i in range(4)]
    for t0, nt in ffn_chunks(DFF):
        for q in range(0, nt, 2):
            plan += [wblock(w_, 0, KD, (t0 + q) * P, 256) for w_ in (w_gate, w_up)]
        plan += [wblock(w_down, t0 * P, nt, i * 512, 512) for i in range(2)]
    w3 = lambda c0, n: w_in2[:, c0:c0 + n].rearrange("(k p) c -> p k c", p=P)
    kpe0 = QLORA + KVLORA
    plan += [wblock(w_in2, 0, KD, 0, 256), wblock(w_in2, 0, KD, 256, 256),
             (KD, 256, [(0, w3(512, P))] + [piece for c0 in (128, 192) for piece in (
                 (c0, w3(kpe0, QR)), (c0 + 32, w3(kpe0 + 16, 16)), (c0 + 48, w3(kpe0, 16)))])]
    plan += [wblock(w_in2, 0, KD, MLA_COLS + RWKV_COLS + 256 * i, 256) for i in range(8)]
    plan += [wblock(w_in2, 0, KD, MLA_COLS + 256 * i, 256) for i in range(RWKV_COLS // 256)]
    run1 = ExitStack()
    gg = sb(run1, "gg", [P, KD], F32, "right")
    op_hi = sb(run1, "op_hi", [P, KD, L], F32R, "right")
    op_lo = sb(run1, "op_lo", [P, KD, L], F32R, "right")
    weights = Weights(run1, plan, raw=2, side="right")

    with ExitStack() as ctx:
        yT = u_tok[:].rearrange("p g j h -> p (g j h)").rearrange("p (k t) -> p k t", k=4)
        y_flat = y_tok[:].rearrange("p j g h -> p (j g h)")
        yT_view = yT.rearrange("p k (c j) -> p k j c", j=SJ)
        y_ready, g_ready = [], {}
        for k in range(4):
            tile_ready = []
            for part in range(2):
                n, ps, free = banks.take()
                for i in range(4):
                    m = transpose(ps[:, i * P:(i + 1) * P],
                                  y_tok[:, part * 4 + i, 8 * k:8 * k + 8, :].rearrange("p g h -> p (g h)"),
                                  free)
                m = copy(evac_engine(part), yT_view[:, k, part * 4:part * 4 + 4, :],
                         ps[:].rearrange("p (j c) -> p j c", j=4), m)
                banks.release(n, m)
                tile_ready.append(m)
            y_ready += tile_ready
            m = act(op_hi[:, k, :], yT[:, k, :], ACT.Copy, tile_ready)
            g_ready[k] = [m, tt(V, op_lo[:, k, :], yT[:, k, :], op_hi[:, k, :], ALU.subtract, m, tile_ready)]
        gate_tmp = y_flat[:, 2 * L:4 * L].rearrange("p (b t) -> p b t", b=4)
        gate_at, gate_free, y_parts = [0], [y_ready] * 4, {}

        def to_glu(i, half, ps, m):
            b = gate_at[0] = (gate_at[0] + 1) % 4
            t = gate_tmp[:, b, :]
            m1 = act(t, ps[:], ACT.Sigmoid, m, gate_free[b], bias=vec["b_glu"][:, i:i + 1])
            m = tt(V, t, t, yT[:, i, hs(half)], ALU.mult, m1)
            m2 = act(op_hi[:, 4 + i, hs(half)], t, ACT.Copy, m)
            m3 = tt(V, op_lo[:, 4 + i, hs(half)], t, op_hi[:, 4 + i, hs(half)], ALU.subtract, m2)
            gate_free[b] = [m2, m3]
            y_parts.setdefault(4 + i, []).extend([m2, m3])
            return [m1]

        glu_read = linear(weights, (op_hi, op_lo), 4, [(i * P, i) for i in range(4)], to_glu, g_ready)

        for i in range(len(WINDOWS)):
            scale = vec["pool_scale"][:, i:i + 1]
            for half in range(2):
                n, ps, free = banks.take()
                m = mm(ps[:], w_pool[:, i, :], u_pool[:, i, hs(half)], True, True, pooled, free, pool_here)
                m1 = act(op_hi[:, i, hs(half)], ps[:], ACT.Copy, m, glu_read, scale=scale)
                m2 = stt(op_lo[:, i, hs(half)], ps[:], scale, op_hi[:, i, hs(half)], ALU.mult, ALU.subtract, m1,
                         glu_read)
                banks.release(n, m1, m2)
                y_parts.setdefault(i, []).extend([m1, m2])
    fence(Q)
    y_closed = now()
    y_ctx.close()
    u_ctx.close()

    def residual_of(hT, then=None, waits=()):
        def to_residual(i, half, ps, m):
            m = tt(V, hT[:, i, hs(half)], hT[:, i, hs(half)], ps[:], ALU.add, m, *waits)
            if half == 1 and then is not None:
                then(i, m)
            return [m]
        return to_residual

    def split_to(fh, fl, f, i, half, m, free):
        m1 = act(fh[:, i, hs(half)], f, ACT.Copy, m, free)
        return m1, tt(G, fl[:, i, hs(half)], f, fh[:, i, hs(half)], ALU.subtract, m1, m, free)

    def down(weights, parts, nt, ready, to_residual):
        for b in range(2):
            last = linear(weights, parts, nt, [(i * P, 4 * b + i) for i in range(4)], to_residual, ready)
        return last

    nm_ctx = ExitStack()
    nm = new_norm(nm_ctx)
    gates = sb(nm_ctx, "gates", [P, 4, HALF])
    op = (op_hi, op_lo)
    for b in range(4):
        w_read = linear(weights, op, KD, [(0, 2 * b), (P, 2 * b + 1)],
                        residual_of(hT, lambda i, m: nm.add(hT[:, i, :], m)), y_parts)
    op_ready = split_scaled(hT, vec["norm_ffn"], op_hi, op_lo, w_read)
    rs_ready = nm.finish(rs, D)

    rope_dram = dram("rope_scratch", [2, P, L])

    m_gg = tt(V, gg[:], vec["norm_final"], vec["g_mix_2"], ALU.mult)
    with ExitStack() as ctx:
        pos, ang, t1, t2 = (sb(ctx, n_, [P, L], d_)[:] for n_, d_ in
                            (("pos", I32), ("ang", F32), ("t1", F32), ("t2", F32)))
        c_rope = count("rope")
        here = Q.dma(c_rope, pos, a["positions_2"].to_broadcast([P, L]), *y_closed)
        copy(V, ang, pos, here, *y_closed)
        ts(V, ang, ang, inv_freq, None, ALU.mult, None)
        m = sincos(ang, t1, ang, (t1, t2))
        m = ts(V, ang, ang, rope_sign, None, ALU.mult, None, *m)
        Q.dma(c_rope, rope_dram[0], t1, m)
        f_read = Q.dma(c_rope, rope_dram[1], ang)
    with ExitStack() as ctx:
        f_hi = sb(ctx, "f_hi", [P, FC, L], F32R)
        f_lo = sb(ctx, "f_lo", [P, FC, L], F32R)
        gate_sb = [gates[:, i, :] for i in range(4)]
        gate_ready, gate_free = [None] * 4, [None] * 4
        V.wait(f_read)
        h_tmp = [sb(ctx, "h_tmp", [P, HALF]) for _ in range(2)]
        f_free = [None, None]
        S.wait(rs_ready), V.wait(rs_ready)
        f_ready = {}

        def to_gate(i, half, ps, m):
            s_ = (i % 2) * 2 + half
            m = tt(V, gate_sb[s_], ps[:], rs[:, hs(half)], ALU.mult, m, gate_free[s_])
            gate_ready[s_] = act(gate_sb[s_], gate_sb[s_], ACT.Silu, m)
            return [m]

        def to_hidden(i, half, ps, m):
            s_ = (i % 2) * 2 + half
            t = h_tmp[half][:]
            m = tt(V, t, ps[:], rs[:, hs(half)], ALU.mult, m, f_free[half])
            m1 = gate_free[s_] = tt(V, t, t, gate_sb[s_], ALU.mult, gate_ready[s_])
            f_free[half] = list(split_to(f_hi, f_lo, t, i, half, m1, f_read))
            f_ready.setdefault(i, []).extend(f_free[half])
            return [m]

        nm2 = Norm(nm.sq, gates[:, 0:2, :].rearrange("p a t -> p (a t)"), nm.read)
        next_ready = {}

        def next_operand(i, m):
            next_ready[i] = split_tile(i, hT[:, i, :], gg[:, i:i + 1], op_hi, op_lo, m, m_gg, up_read)
            nm.add(hT[:, i, :], m)
            nm2.add(hT[:, i, :], m, gate_free, scale=vec["norm_final"][:, i:i + 1], engine=V)

        chunks = ffn_chunks(DFF)
        for t0, nt in chunks:
            f_ready = {}
            for q in range(0, nt, 2):
                linear(weights, op, KD, [(0, q), (P, q + 1)], to_gate, op_ready)
                up_read = linear(weights, op, KD, [(0, q), (P, q + 1)], to_hidden, op_ready)
            f_read = down(weights, (f_hi, f_lo), nt, f_ready,
                          residual_of(hT, next_operand if t0 == chunks[-1][0] else None))
        s1, s2, t_ = (ncol[:, i, :] for i in range(3))
        m = nm.columns(s1)
        m2 = nm2.columns(s2)
        m = act(s1, s1, ACT.Sqrt, m, bias=eps_col, scale=1.0 / D)
        m_rs1 = V.do(lambda e: e.reciprocal(s1, s1), m)
        tt(V, t_, s1, s1, ALU.mult)
        m = stt(s2, s2, 1.0 / D, t_, ALU.mult, ALU.mult, m2)
        m = act(s2, s2, ACT.Sqrt, m, bias=eps_col)
        V.do(lambda e: e.reciprocal(s2, s2), m)
        m = tt(V, s2, s2, s1, ALU.mult)
        rs_ready = spread(rs, s2, m)
        rs1 = gates[:, 2:4, :].rearrange("p a t -> p (a t)")
        rs1_ready = spread(rs1, s1, m, gate_free)
    op_ready = next_ready
    streams_now = [(s_.done, s_.done.value) for s_ in (V, S, G, T)]
    for s_ in (V, S, G, Q):
        s_.wait(streams_now)
    Z_KPE, Z_RWKV, Z_GATE = QLORA + KVLORA, QLORA + KVLORA + P, QLORA + KVLORA + P + RWKV_COLS

    def z_tile(row, half=None):
        t = z_dram[row:row + P, :]
        return t if half is None else t[:, hs(half)]

    with ExitStack() as ctx:
        store = Ring([sb(ctx, "z_out", [P, HALF]) for _ in range(2)], [count(f"z_out{i}") for i in range(2)])
        with ExitStack() as mctx:
            lat = sb(mctx, "lat", [P, 5, L])
            cos_sin = sb(mctx, "cos_sin", [P, L])
            lat_rs = sb(mctx, "lat_rs", [P, L])
            nm_kv = Norm(nm.sq, sb(mctx, "sq_sum_kv", [P, L]), nm.read)
            Q.dma(c_rope, cos_sin[64:96, :], rope_dram[0, 64:96])
            rope_here = Q.dma(c_rope, cos_sin[96:128, :], rope_dram[1, 96:128])
            kpe = gates[:, 0:2, :].rearrange("p a t -> p (a t)")
            c_lat = count("latent_out")

            def to_latent(i, half, ps, m):
                if i == 5:
                    return [tt(V, kpe[:, hs(half)], ps[:], rs[:, hs(half)], ALU.mult, m)]
                m = tt(V, lat[:, i, hs(half)], ps[:], rs[:, hs(half)], ALU.mult, m)
                if half == 1:
                    (nm if i < 3 else nm_kv).add(lat[:, i, :], m)
                return [m]

            def scale_latent(nm_, kt, k0, n_ch, g, *marks):
                ready = nm_.finish(lat_rs, n_ch, *marks)
                for k in range(kt):
                    m = stt(lat[:, k0 + k, :], lat[:, k0 + k, :], g[:, k:k + 1], lat_rs[:], ALU.mult, ALU.mult,
                            ready)
                Q.dma(c_lat, z_dram[k0 * P:(k0 + kt) * P, :].rearrange("(k p) t -> p k t", p=P),
                      lat[:, k0:k0 + kt, :], m)
                return m

            for b in range(3):
                linear(weights, op, KD, [(0, 2 * b), (P, 2 * b + 1)], to_latent, op_ready)
                if b == 0:
                    for k in range(KD):
                        m = stt(hT[:, k, :], hT[:, k, :], vec["norm_final"][:, k:k + 1], rs1, ALU.mult, ALU.mult,
                                next_ready[k], rs1_ready)
                    Q.dma(count("x_keep"), x_dram.rearrange("(k p) t -> p k t", p=P), hT[:], m)
            q_scaled = scale_latent(nm, 3, 0, QLORA, vec["g_q_a_2"])
            m = tt(V, cos_sin[64:128, :], kpe[64:128, :], cos_sin[64:128, :], ALU.mult, rope_here)
            m = copy(G, kpe[64:96, :], cos_sin[96:128, :], m)
            m = tt(G, kpe[64:96, :], kpe[64:96, :], cos_sin[64:96, :], ALU.add)
            Q.dma(c_lat, z_dram[Z_KPE:Z_KPE + 32, :], kpe[64:96, :], m)

            def to_gates(i, half, ps, m):
                s_, t, free = store.take()
                m = tt(V, t[:], ps[:], rs[:, hs(half)], ALU.mult, m, free)
                m1 = act(t[:], t[:], ACT.Sigmoid, m)
                store.release(s_, Q.dma(store.counts[s_], z_tile(Z_GATE + i * P, half), t[:], m1))
                return [m]

            for b in range(8):
                linear(weights, op, KD, [(0, 2 * b), (P, 2 * b + 1)], to_gates, op_ready)
                if b == 0:
                    scale_latent(nm_kv, 2, 3, KVLORA, vec["g_kv_a_2"], q_scaled)
            streams_now = now()
            for s_ in (V, S, G):
                s_.wait(streams_now)
        rows = [sb(ctx, "z_row", [P, L + 1]) for _ in range(2)]
        shifted = Ring([sb(ctx, "z_shift", [P, L]) for _ in range(2)], [count(f"zs_out{i}") for i in range(2)])
        for t in rows:
            V.do(lambda e, t=t: e.memset(t[:, 0:1], 0.0))

        def to_rwkv(i, half, ps, m):
            row_, mu = rows[i % 2], vec["mu_rwkv_2"][:, i:i + 1]
            m = tt(V, row_[:, 1 + half * HALF:1 + half * HALF + HALF], ps[:], rs[:, hs(half)], ALU.mult, m)
            if half == 1:
                s_, t, free = shifted.take()
                tt(V, t[:], row_[:, 0:L], row_[:, 1:L + 1], ALU.subtract, free)
                m1 = stt(t[:], t[:], mu, row_[:, 1:L + 1], ALU.mult, ALU.add)
                shifted.release(s_, Q.dma(shifted.counts[s_], z_tile(Z_RWKV + i * P), t[:], m1))
            return [m]

        for b in range(7):
            linear(weights, op, KD, [(0, 2 * b), (P, 2 * b + 1)], to_rwkv, op_ready)
    fence()
    nm_ctx.close()
    run1.close()
    res.close()
    xs_dram = dram("own_scratch", [2, NPAIR, P, NC, C])
    yw = ExitStack()
    y_wkv = sb(yw, "y_wkv", [P, NPAIR, L])
    heads = (slice(0, 64), slice(64, 128))
    halves = tuple((slice(h.start, h.start + HC), slice(h.start + HC, h.stop)) for h in heads)
    with ExitStack() as ctx:
        c_rw = count("rwkv_in")
        ar = sb(ctx, "ar", [P, NPAIR, NC, 2, C])
        score_rb = sb(ctx, "score_rb", [P, NPAIR, NC, C])
        inv = sb(ctx, "inv", [P, NPAIR, NC, C])
        b_hat = sb(ctx, "b_hat", [P, NPAIR, NC, C])
        chunk_decay = sb(ctx, "chunk_decay", [P, NPAIR, NC])
        c_n = [count(f"n_out{i}") for i in range(NPAIR)]
        with ExitStack() as tctx:
            lo_rank = sb(tctx, "lo_rank", [P, L])
            g_rank = sb(tctx, "g_rank", [P, L])
            w2a2 = sb(tctx, "w2a2", [P, 512])
            g2 = sb(tctx, "g2", [P, 512])
            wkv_mask = sb(tctx, "wkv_mask", [P, 2 * C])
            chunk_mask = sb(tctx, "chunk_mask", [P, L])
            Q.dma(c_rw, lo_rank[:], z_tile(Z_RWKV + 1536))
            Q.dma(c_rw, g_rank[:], z_tile(Z_RWKV + 1664))
            Q.dma(c_rw, w2a2[0:64, :], a["w2_2"][0])
            Q.dma(c_rw, w2a2[64:128, :], a["a2_2"][0])
            Q.dma(c_rw, g2[:], a["g2_2"][0])
            Q.dma(c_rw, wkv_mask[:], a["k_wkv_mask"])
            here = Q.dma(c_rw, chunk_mask[:], a["k_chunk_mask"])
            m = act(lo_rank[0:64, :], lo_rank[0:64, :], ACT.Tanh, here)
            ranks = act(g_rank[:], g_rank[:], ACT.Sigmoid, m)
            tile = lambda name: sb(tctx, name, [P, L])
            r_, k_, kk, t2 = (tile(n_) for n_ in ("r", "k", "kk", "t2"))
            sets = [[tile(n_) for n_ in ("sg", "cs", "ea", "eb", "v", "a", "t1")] for _ in range(2)]
            k_score = sb(tctx, "k_score", [P, NC // 2, 2, C])
            x_ring = Ring([sb(tctx, "x_pair", [P, NC, C])], [count("x_out")])
            s_ring = Ring([sb(tctx, "s_pair", [P, NC, C])], [count("s_out")])
            c_p = [count(f"pair_in{i}") for i in range(3)]
            c_o = [count(f"pair_out{i}") for i in range(2)]
            by_chunk = lambda t: t[:].rearrange("p (c t) -> p c t", t=C)
            mask2 = wkv_mask[:].rearrange("p (a t) -> p a t", a=2)
            over_c = lambda v: v.unsqueeze(1).to_broadcast([P, 4, C])
            n_view = n_dram.rearrange("(p h c) (d s t) -> p h d s c t", p=NPAIR, h=2, d=2, s=HC)
            front_done, back_done, at_pair, k_read = {}, {}, {}, [None]

            def front(p):
                pc = slice(p * P, (p + 1) * P)
                col = lambda name: vec[name][:, p:p + 1]
                sg, cs, ea, eb, v_, a_, t1 = sets[p % 2]
                before = [front_done.get(p - 1, []), back_done.get(p - 2, [])]
                r_here = Q.dma(c_p[0], r_[:], z_tile(Z_RWKV + p * P), *before)
                k_here = Q.dma(c_p[1], k_[:], z_tile(Z_RWKV + 512 + p * P))
                v_here = Q.dma(c_p[2], v_[:], z_tile(Z_RWKV + 1024 + p * P))
                for half in range(2):
                    n, ps, free = banks.take()
                    m = mm(ps[:], w2a2[0:64, pc], lo_rank[0:64, hs(half)], True, True, ranks, free)
                    m_sg = act(sg[:, hs(half)], ps[:], ACT.Sigmoid, m, *before, bias=col("w0_2"))
                    banks.release(n, m_sg)
                    n, ps, free = banks.take()
                    m = mm(ps[:], w2a2[64:128, pc], lo_rank[64:128, hs(half)], True, True, free)
                    m_a = act(a_[:, hs(half)], ps[:], ACT.Sigmoid, m, *before, bias=col("a0_2"))
                    banks.release(n, m_a)
                    yield 1
                    n, ps, free = banks.take()
                    m = mm(ps[:], g2[:, pc], g_rank[:, hs(half)], True, True, free)
                    m_g = copy(S, t2[:, hs(half)], ps[:], m, *before)
                    banks.release(n, m_g)
                    yield 1
                g_out = Q.dma(c_o[0], g_dram[pc, :], t2[:], m_g)
                ts(V, kk[:], k_[:], col("k_k_2"), None, ALU.mult, None, k_here, *before)
                m = tt(V, t1[:], kk[:], kk[:], ALU.mult)
                yield 2
                for half in range(2):
                    n, ps, free = banks.take()
                    m1 = mm(ps[:], headones[:], t1[:, hs(half)], True, True, m, free)
                    m2 = act(eb[:, hs(half)], ps[:], ACT.Sqrt, m1, *before)
                    banks.release(n, m2)
                yield 2
                m_cs = V.do(lambda e: e.tensor_tensor_scan(cs[:], chunk_mask[:], sg[:], 0.0, ALU.mult, ALU.add),
                            here, m_sg)
                ts(V, eb[:], eb[:], 1e-12, None, ALU.max, None, m2)
                V.do(lambda e: e.reciprocal(eb[:], eb[:]))
                m_kk = tt(V, kk[:], kk[:], eb[:], ALU.mult)
                yield 9
                ts(V, t1[:], a_[:], -1.0, col("k_a_2"), ALU.add, ALU.mult, m_a, m1)
                stt(k_[:], t1[:], 1.0, k_[:], ALU.add, ALU.mult)
                yield 2
                m = stt(t1[:], r_[:], col("r_k_2"), k_[:], ALU.mult, ALU.mult, r_here)
                for half in range(2):
                    n, ps, free = banks.take()
                    m_t1 = mm(ps[:], headones[:], t1[:, hs(half)], True, True, m, free)
                    m2 = tt(V, t2[:, hs(half)], ps[:], v_[:, hs(half)], ALU.mult, m_t1, v_here, g_out)
                    banks.release(n, m2)
                bonus_out = Q.dma(c_o[1], bonus_dram[pc, :], t2[:], m2)
                yield 4
                m1 = act(ea[:], cs[:], ACT.Exp, m_cs, scale=-DECAY)
                m = tt(V, sg[:], cs[:], sg[:], ALU.subtract)
                m2 = act(eb[:], sg[:], ACT.Exp, m, m_kk, scale=-DECAY)
                at_view, rt_view = ar[:, p, :, 0, :], ar[:, p, :, 1, :]
                tt(V, rt_view, by_chunk(r_), by_chunk(ea), ALU.mult, m1)
                yield 3
                copy(V, chunk_decay[:, p, :], by_chunk(ea)[:, :, C - 1])
                m_ar = stt(at_view, by_chunk(kk), -1.0, by_chunk(eb), ALU.mult, ALU.mult, m2)
                m_kka = tt(V, kk[:], kk[:], a_[:], ALU.mult)
                yield 4
                m1 = act(ea[:], cs[:], ACT.Exp, m_ar, scale=DECAY)
                end = by_chunk(cs)[:, :, C - 1:C].to_broadcast([P, NC, C])
                m_e = tt(V, by_chunk(t1), by_chunk(cs), end, ALU.subtract, m_t1)
                m2 = act(eb[:], t1[:], ACT.Exp, m_e, m_ar, scale=DECAY)
                yield 4
                m_bt = tt(V, sg[:], kk[:], ea[:], ALU.mult, m1)
                m_kt = tt(V, cs[:], k_[:], ea[:], ALU.mult, m_e)
                yield 4
                m_bh = tt(V, a_[:], kk[:], eb[:], ALU.mult, m2)
                m_kh = tt(V, t1[:], k_[:], eb[:], ALU.mult)
                yield 4
                at_pair[p] = (m_bt, m_ar, m_kt, m_bh, m_kh)
                front_done[p] = [(s_.done, s_.done.value) for s_ in (V, S, T)] + [bonus_out]

            def back(p):
                m_bt, m_ar, m_kt, m_bh, m_kh = at_pair[p]
                sg, cs, ea, eb, v_, a_, t1 = sets[p % 2]
                for src, dst, m_src in ((a_, b_hat[:, p, :, :], m_bh), (t1, by_chunk(ea), m_kh),
                                        (v_, by_chunk(eb), m_kh)):
                    for q in range(2):
                        n, ps, free = banks.take()
                        for i in range(8):
                            c = q * 8 + i
                            for h in heads:
                                m = mm(ps[h, i * C:(i + 1) * C], src[h, c * C:(c + 1) * C], ident[h, h],
                                       True, True, m_src, free, signal=(i == 7 and h is heads[1]))
                        m = copy(S, dst[:, q * 8:q * 8 + 8, :], ps[:].rearrange("p (c t) -> p c t", c=8), m, m_kh)
                        banks.release(n, m)
                        yield
                m_rows = m
                khs, vs = by_chunk(ea), by_chunk(eb)
                for q in range(4):
                    n, ps, free = banks.take()
                    for i in range(4):
                        c = q * 4 + i
                        for h in heads:
                            m = mm(ps[h, i * P:(i + 1) * P], sg[h, c * C:(c + 1) * C],
                                   ar[h, p, c, :, :].rearrange("p a t -> p (a t)"), True, True, m_bt, m_ar, free,
                                   signal=(i == 3 and h is heads[1]))
                    v4 = ps[:].rearrange("p (c a t) -> p c a t", c=4, a=2)
                    cq = slice(q * 4, q * 4 + 4)
                    tt(V, inv[:, p, cq, :], v4[:, :, 0, :], over_c(mask2[:, 0, :]), ALU.mult, m)
                    m_n = tt(V, score_rb[:, p, cq, :], v4[:, :, 1, :], over_c(mask2[:, 1, :]), ALU.mult)
                    banks.release(n, m_n)
                    yield
                for i_h in range(2):
                    for d, part in enumerate(halves[i_h]):
                        Q.dma(c_n[p], n_view[p, i_h, d], inv[part, p, :, d * HC:(d + 1) * HC], m_n)
                nx, x_t, x_free = x_ring.take()
                ns, s_t, s_free = s_ring.take()
                for q8 in range(2):
                    for q in range(2):
                        n, ps, free = banks.take()
                        for i in range(4):
                            c = q8 * 8 + q * 4 + i
                            for h in heads:
                                m = mm(ps[h, i * P:(i + 1) * P], cs[h, c * C:(c + 1) * C],
                                       ar[h, p, c, :, :].rearrange("p a t -> p (a t)"), True, True, m_kt, m_ar,
                                       free, signal=(i == 3 and h is heads[1]))
                        m_ks = V.do(lambda e, o=k_score[:, q * 4:q * 4 + 4, :, :].rearrange("p c a t -> p c (a t)"),
                                    x=ps[:].rearrange("p (c n) -> p c n", c=4),
                                    y=wkv_mask[:].unsqueeze(1).to_broadcast([P, 4, P]):
                                    e.tensor_tensor(o, x, y, ALU.mult), m, k_read[0])
                        banks.release(n, m_ks)
                        yield
                    c8 = slice(q8 * 8, q8 * 8 + 8)
                    for kind in range(3):
                        n, ps, free = banks.take()
                        for i in range(8):
                            c = q8 * 8 + i
                            for h in heads:
                                w, x = ((k_score[h, i, 0, :], vs[h, c, :]), (vs[h, c, :], k_score[h, i, 1, :]),
                                        (khs[h, c, :], vs[h, c, :]))[kind]
                                m = mm(ps[h, i * C:(i + 1) * C], w, x, True, True, m_ks, m_rows, free,
                                       signal=(i == 7 and h is heads[1]))
                        dst = (x_t[:, c8, :], y_wkv[:, p, q8 * HALF:(q8 + 1) * HALF].rearrange(
                            "p (c t) -> p c t", c=8), s_t[:, c8, :])[kind]
                        m1 = copy(S, dst, ps[:].rearrange("p (c t) -> p c t", c=8), m, x_free, s_free)
                        banks.release(n, m1)
                        yield
                    k_read[0] = m
                x_ring.release(nx, Q.dma(x_ring.counts[nx], xs_dram[0, p], x_t[:], m1))
                s_ring.release(ns, Q.dma(s_ring.counts[ns], xs_dram[1, p], s_t[:], m1))
                back_done[p] = [(T.done, T.done.value)]

            for _ in front(0):
                pass
            for p in range(NPAIR):
                ahead = front(p + 1) if p + 1 < NPAIR else iter(())
                owed = 0
                for _ in back(p):
                    owed += 42 / 20
                    while owed > 0:
                        cost = next(ahead, None)
                        if cost is None:
                            break
                        owed -= cost
                for _ in ahead:
                    pass
        fence()
        x_own = sb(ctx, "x_own", [P, NPAIR, NC, C])
        s_own = sb(ctx, "s_own", [P, NPAIR, NC, C])
        c_own = count("own_in")
        for i, t in enumerate((x_own, s_own)):
            for p in range(NPAIR):
                Q.dma(c_own, t[:, p, :, :], xs_dram[i, p])

        with ExitStack() as tctx:
            nu = sb(tctx, "nu", [P, 2, HC, HC])
            ru = sb(tctx, "ru", [P, 2, HC, HC])
            ra_turned = sb(tctx, "ra_turned", [P, HC, HC])
            tmp_v = sb(tctx, "tmp_v", [P, 2, HC * HC // 4])
            ra_t = sb(tctx, "ra_t", [P, NPAIR, NC, HC])
            z_t = sb(tctx, "z_t", [P, NPAIR, NC, HC])
            c_u = count("units")
            here = Q.dma(c_u, nu[:].rearrange("p d s t -> p (d s t)"), n_dram)
            p_tok = sb(tctx, "p_tok", [P, SJ, 256])
            pT = sb(tctx, "pT", [P, 2, L])
            w_proj = sb(tctx, "w_proj", [P, 2, D])
            c_ple = count("ple_in")
            Q.dma(c_ple, p_tok[:], a["p_2"][0, 0].rearrange("(t p) d -> p t d", p=P))
            p_here = Q.dma(c_ple, w_proj[:], a["w_ple_proj_2"][0].rearrange("(k p) c -> p k c", p=P))
            for k in range(2):
                for q in range(2):
                    n, ps, free = banks.take()
                    for i in range(4):
                        m = transpose(ps[:, i * P:(i + 1) * P], p_tok[:, q * 4 + i, k * P:(k + 1) * P], p_here,
                                      free)
                    m_pT = copy(S, pT[:, k, hs(q)], ps[:], m)
                    banks.release(n, m_pT)
            store = Ring([sb(tctx, "proj_out", [P, HALF]) for _ in range(2)],
                         [count(f"proj_out{i}") for i in range(2)])
            for i in range(KD):
                for half in range(2):
                    n, ps, free = banks.take()
                    m = product(ps[:], [(w_proj[:, k, i * P:(i + 1) * P], pT[:, k, hs(half)]) for k in range(2)],
                                m_pT, free)
                    s_, t, free = store.take()
                    m = copy(S, t[:], ps[:], m, free)
                    banks.release(n, m)
                    store.release(s_, Q.dma(store.counts[s_], proj_dram[i * P:(i + 1) * P, hs(half)], t[:], m))
            V.do(lambda e: e.memset(ru[:], 0.0))
            m = V.do(lambda e: e.memset(ru[:].rearrange("p d s t -> p d (s t)")[:, :, 0:HC * HC:HC + 1], 1.0), here)
            for s_ in range(HC - 1):
                i_n, t_n = s_ + 1, HC - 1 - s_
                shape = [P, 2, i_n, t_n]
                tv = tmp_v[:, :, 0:i_n * t_n].rearrange("p d (i t) -> p d i t", i=i_n)
                tt(V, tv, ru[:, :, 0:i_n, s_:s_ + 1].to_broadcast(shape),
                   nu[:, :, s_:s_ + 1, s_ + 1:HC].to_broadcast(shape), ALU.mult)
                m = tt(V, ru[:, :, 0:i_n, s_ + 1:HC], ru[:, :, 0:i_n, s_ + 1:HC], tv, ALU.add)
            r_out = Q.dma(c_u, r_dram, ru[:].rearrange("p d s t -> p (d s t)"), m)
            m = copy(V, ra_turned[:], ru[:, 0].rearrange("p i s -> p s i"))
            rt_out = Q.dma(count("turned_out"), rt_dram, ra_turned[:].rearrange("p s i -> p (s i)"), m)
            r_view = r_dram.rearrange("(p h c) (d s t) -> p h d s c t", p=NPAIR, h=2, d=2, s=HC)
            rt_view = rt_dram.rearrange("(p h c) (s i) -> p h s c i", p=NPAIR, h=2, s=HC)
            c_r = [count(f"r_in{p}") for p in range(NPAIR)]
            for p in range(NPAIR):
                for i_h in range(2):
                    upper, lower = halves[i_h]
                    Q.dma(c_r[p], ra_t[upper, p, :, :], rt_view[p, i_h], rt_out)
                    Q.dma(c_r[p], inv[upper, p, :, 0:HC], r_view[p, i_h, 0], r_out)
                    r_here = Q.dma(c_r[p], inv[lower, p, :, HC:C], r_view[p, i_h, 1])
                n, ps, free = banks.take()
                for c in range(NC):
                    for upper, lower in halves:
                        m = mm(ps[lower, c * HC:(c + 1) * HC], inv[upper, p, c, HC:C], ra_t[upper, p, c, :], True,
                               True, r_here, free, signal=(c == NC - 1 and lower is halves[1][1]))
                z_ready = []
                for eng, (_, lower) in zip((V, S), halves):
                    z_ready.append(copy(eng, z_t[lower, p, :, :], ps[lower, :].rearrange("p (c i) -> p c i", c=NC), m))
                banks.release(n, *z_ready)
                n, ps, free = banks.take()
                for c in range(NC):
                    for upper, lower in halves:
                        m = mm(ps[upper, c * HC:(c + 1) * HC], z_t[lower, p, c, :], inv[lower, p, c, HC:C], True,
                               True, z_ready, free, signal=(c == NC - 1 and lower is halves[1][1]))
                ends = []
                for eng, (upper, _) in zip((V, S), halves):
                    ends.append(copy(eng, inv[upper, p, :, HC:C], ps[upper, :].rearrange("p (c i) -> p c i", c=NC), m))
                banks.release(n, *ends)
        fence()

        s_now = [sb(ctx, "s_now", [P, NPAIR, C]) for _ in range(2)]
        us = [sb(ctx, "us", [P, NPAIR, C]) for _ in range(2)]
        s_dec = sb(ctx, "s_dec", [P, NPAIR, C])
        xs = sb(ctx, "xs", [P, NPAIR, C])
        m_s = V.do(lambda e: e.memset(s_now[0][:], 0.0))
        y_view = y_wkv[:].rearrange("p n (c t) -> p n c t", t=C)
        blk = lambda v: v.rearrange("p (n t) -> p n t", n=NPAIR)

        def every_head(w_of, x_of, *marks):
            n, ps, free = banks.take()
            for p in range(NPAIR):
                for h in heads:
                    m = mm(ps[h, p * C:(p + 1) * C], w_of(p, h), x_of(p, h), True, True, *marks, free,
                           signal=(p == NPAIR - 1 and h is heads[1]))
            return n, blk(ps[:, 0:256]), m

        def add_y(c, n, v, m):
            m = tt(V, y_view[:, :, c, :], y_view[:, :, c, :], v, ALU.add, m)
            banks.release(n, m)

        def y_of_u(c):
            u_ = us[c % 2]
            return every_head(lambda p, h: u_[h, p, :], lambda p, h: score_rb[h, p, c, :])

        y_u = None
        for c in range(NC):
            s_old, s_new, u_ = s_now[c % 2], s_now[1 - c % 2], us[c % 2]
            nx, x_ps, m_x = every_head(lambda p, h: ar[h, p, c, 0, :], lambda p, h: s_old[h, p, :], m_s)
            ny, y_ps, m_y = every_head(lambda p, h: s_old[h, p, :], lambda p, h: ar[h, p, c, 1, :])
            m_xs = tt(V, xs[:], x_ps, x_own[:, :, c, :], ALU.add, m_x)
            banks.release(nx, m_xs)
            decay = chunk_decay[:, :, c].unsqueeze(2).to_broadcast([P, NPAIR, C])
            tt(G, s_dec[:], s_old[:], decay, ALU.mult, m_s)
            m_dec = tt(G, s_dec[:], s_dec[:], s_own[:, :, c, :], ALU.add)
            nu_, u_ps, m_u = every_head(lambda p, h: inv[h, p, c, :], lambda p, h: xs[h, p, :], m_xs)
            add_y(c, ny, y_ps, m_y)
            if y_u is not None:
                add_y(*y_u)
            m_us = copy(V, u_[:], u_ps, m_u)
            banks.release(nu_, m_us)
            ns, s_ps, m_sp = every_head(lambda p, h: b_hat[h, p, c, :], lambda p, h: u_[h, p, :], m_us)
            m_s = tt(V, s_new[:], s_ps, s_dec[:], ALU.add, m_sp, m_dec)
            banks.release(ns, m_s)
            y_u = (c, *y_of_u(c))
        add_y(*y_u)
    fence()

    mixb_dram = dram("mixb_scratch", [D, L])
    with ExitStack() as ctx:
        weights = Weights(ctx, [wblock(a["w_o_rwkv_2"][0], 0, 4, i * 512, 512) for i in range(2)], raw=2, parts=1)
        hi = sb(ctx, "yr_hi", [P, 4, L], F32R)
        lo = sb(ctx, "yr_lo", [P, 4, L], F32R)
        gb = sb(ctx, "gb", [P, 4, L])
        bonus = sb(ctx, "bonus", [P, 4, L])
        sqs, rstds = ([sb(ctx, n_, [P, L]) for _ in range(2)] for n_ in ("sq", "rstd"))
        c_g = count("gate_bonus_in")
        Q.dma(c_g, gb[:], g_dram.rearrange("(k p) t -> p k t", p=P))
        here = Q.dma(c_g, bonus[:], bonus_dram.rearrange("(k p) t -> p k t", p=P))
        gin = Ring([sb(ctx, "gate_in", [P, HALF]) for _ in range(4)], [count(f"gb_in{i}") for i in range(4)])
        gates_b = [(i, half) for i in range(KD) for half in range(2)]
        gate_here = {}

        def load_gate():
            if gates_b:
                i, half = gates_b.pop(0)
                s_, g, free = gin.take()
                gate_here[i, half] = (s_, g, Q.dma(gin.counts[s_], g[:], z_tile(Z_GATE + D + i * P, half), free))

        for _ in range(4):
            load_gate()
        plan = []
        wuq, wukv = a["w_uq_2"][0], a["w_ukv_2"][0]
        w3 = lambda w, c0, n: w[:, c0:c0 + n].rearrange("(k p) c -> p k c", p=P)
        for b in range(2):
            pieces = []
            for i in range(4):
                c0 = (4 * b + i) * QH
                pieces += [(i * P, w3(wuq, c0, QH)), (i * P + QH, w3(wuq, c0 + QN + 16, 16)),
                           (i * P + QH + 16, w3(wuq, c0 + QN, 16))]
            plan.append((3, 512, pieces))
        plan.append(wblock(wukv, 0, 2, 0, 1024))
        mla_ctx = ExitStack()
        mla_weights = Weights(mla_ctx, plan, raw=2, parts=1, side="right")
        cin = sb(mla_ctx, "latents", [P, 5, L], F32, "right")
        c_m = [count(f"mla_in{i}") for i in range(4)]
        q_here = Q.dma(c_m[2], cin[:, 0:3, :], z_dram[0:QLORA, :].rearrange("(k p) t -> p k t", p=P))
        kv_here = Q.dma(c_m[3], cin[:, 3:5, :],
                        z_dram[QLORA:QLORA + KVLORA, :].rearrange("(k p) t -> p k t", p=P))
        used = {-2: None, -1: None}
        var, yr_ready = {}, {}

        def centre(k):
            y, sq, rstd = y_wkv[:, k, :], sqs[k % 2], rstds[k % 2]
            for half in range(2):
                n, ps, free = banks.take()
                m = mm(ps[:], headones[:], y[:, hs(half)], True, True, free)
                m1 = stt(y[:, hs(half)], ps[:], -1.0 / 64, y[:, hs(half)], ALU.mult, ALU.add, m)
                banks.release(n, m1)
            m = act(sq[:], y, ACT.Square, m1, used[k - 2])
            for half in range(2):
                n, ps, free = banks.take()
                m1 = mm(ps[:], headones[:], sq[:, hs(half)], True, True, m, free)
                var[k] = act(rstd[:, hs(half)], ps[:], ACT.Sqrt, m1, bias=gn_eps_col, scale=1.0 / 64)
                banks.release(n, var[k])

        def scale(k):
            y, rstd = y_wkv[:, k, :], rstds[k % 2]
            V.do(lambda e: e.reciprocal(rstd[:], rstd[:]), var[k])
            used[k] = tt(V, y, y, rstd[:], ALU.mult)
            m = ts(V, y, y, vec["ln_x_w_2"][:, k:k + 1], vec["ln_x_b_2"][:, k:k + 1], ALU.mult, ALU.add)
            m = tt(G, y, y, bonus[:, k, :], ALU.add, m, here)
            m = tt(G, y, y, gb[:, k, :], ALU.mult)
            m1 = act(hi[:, k, :], y, ACT.Copy, m)
            yr_ready[k] = [m1, tt(V, lo[:, k, :], y, hi[:, k, :], ALU.subtract, m1, m)]

        centre(0)
        for k in range(4):
            if k < 3:
                centre(k + 1)
            scale(k)
        store = Ring([sb(ctx, "mix_out", [P, HALF]) for _ in range(4)], [count(f"mb_out{i}") for i in range(4)])

        def to_mix_b(i, half, ps, m):
            s_, g, g_here = gate_here.pop((i, half))
            o_, t, free = store.take()
            m = tt(V, t[:], ps[:], g[:], ALU.mult, m, g_here, free)
            gin.release(s_, m)
            store.release(o_, Q.dma(store.counts[o_], mixb_dram[i * P:(i + 1) * P, hs(half)], t[:], m))
            load_gate()
            return [m]

        for b in range(2):
            linear(weights, (hi, lo), 4, [(i * P, 4 * b + i) for i in range(4)], to_mix_b, yr_ready)
    yw.close()
    fence()
    run3 = ExitStack()
    hT = qT = sb(run3, "hT2", [P, KD, L])
    fctx = ExitStack()
    f_hi, f_lo = (sb(fctx, n_, [P, FC, L], F32R) for n_ in ("f2_hi", "f2_lo"))
    o_ready = {k: [] for k in range(4)}
    scale_qk = QH ** -0.5
    with ExitStack() as ctx:
        kT = sb(ctx, "kT", [P, NH, L])
        v_tok = sb(ctx, "v_tok", [P, SJ, 512])
        with ExitStack() as tctx:
            c_hi = sb(tctx, "c_hi", [P, 3, L], F32R)
            c_lo = sb(tctx, "c_lo", [P, 3, L], F32R)
            weights = mla_weights
            cos_t, sin_t = sb(tctx, "cos_t", [P, L]), sb(tctx, "sin_t", [P, L])
            Q.dma(c_m[0], cos_t[:], rope_dram[0])
            rope_here = Q.dma(c_m[0], sin_t[:], rope_dram[1])
            kpe_here = Q.dma(c_m[1], kT[64:96, 0, :], z_dram[Z_KPE:Z_KPE + 32, :])
            for h in range(1, NH):
                copy((V, S)[h % 2], kT[64:96, h, :], kT[64:96, 0, :], kpe_here)

            def latent(kt, k0, here, *marks):
                ready = {}
                for k in range(kt):
                    m = act(c_hi[:, k, :], cin[:, k0 + k, :], ACT.Copy, here, *marks)
                    ready[k] = [m, tt(V, c_lo[:, k, :], cin[:, k0 + k, :], c_hi[:, k, :], ALU.subtract, m, here,
                                      *marks)]
                return ready

            m_lat = latent(3, 0, q_here)
            rot = [sb(tctx, "rot", [P, HALF]) for _ in range(2)]
            rot_free = [None, None]

            def to_q(h, half, ps, m):
                q, r_ = qT[:, h, hs(half)], rot[half]
                cols = hs(half)
                m1 = act(q[0:64], ps[0:64, :], ACT.Copy, m)
                m2 = tt(V, r_[96:128, :], ps[96:128, :], sin_t[96:128, cols], ALU.mult, m, rot_free[half],
                        rope_here)
                m3 = tt(V, q[64:96], ps[64:96, :], cos_t[64:96, cols], ALU.mult, m)
                m4 = copy(V, r_[64:96, :], r_[96:128, :])
                rot_free[half] = tt(G, q[64:96], q[64:96], r_[64:96, :], ALU.add, m3, m4)
                return [m1, m2, m3]

            for b in range(2):
                q_read = linear(weights, (c_hi, c_lo), 3, [(i * P, 4 * b + i) for i in range(4)], to_q, m_lat)
            whi, wlo, there = weights.take()
            w, x = (whi, wlo), (c_hi, c_lo)
            m_kv = latent(2, 3, kv_here, q_read)
            kv_ready = list(m_kv.values())
            for h in range(NH):
                for half in range(2):
                    n, ps, free = banks.take()
                    m = product(ps[:], three(w, x, 2, slice(h * P, (h + 1) * P), hs(half)), free, there, kv_ready)
                    m = copy(evac_engine(half), kT[0:64, h, hs(half)], ps[0:64, :], m)
                    banks.release(n, m)
            for t in range(SJ):
                n, ps, free = banks.take()
                tok_ = slice(t * P, (t + 1) * P)
                pairs = []
                for k in range(2):
                    wv = [part[:, k, :].rearrange("p (h c) -> p h c", h=NH)[:, :, QN:P] for part in w]
                    pairs += [(x[0][:, k, tok_], wv[0]), (x[0][:, k, tok_], wv[1]), (x[1][:, k, tok_], wv[0])]
                m = product(ps[:].rearrange("p (h c) -> p h c", h=NH), pairs, free)
                m = copy(evac_engine(t), v_tok[:, t, :], ps[:], m)
                banks.release(n, m)
            weights.done(m)
        fence()
        mla_ctx.close()

        plan = [wblock(a["w_o_mla_2"][0], 0, 4, i * 512, 512) for i in range(2)]
        plan += [wblock(w_out2, 0, KD, 256 * i, 256) for i in range(4)]
        w_up2, w_down2 = a["w_ffn_up_2"][0], a["w_ffn_down_2"][0]
        for t0, nt in ffn_chunks(DFF2):
            plan += [wblock(w_up2, 0, KD, (t0 + q) * P, 256) for q in range(0, nt, 2)]
            plan += [wblock(w_down2, t0 * P, nt, i * 512, 512) for i in range(2)]
        plan += [wblock(a["w_ple_gate_2"][0], 0, KD, 256 * i, 256) for i in range(4)]
        weights = Weights(run3, plan, raw=2, side="right")

        with ExitStack() as tctx:
            causal = sb(tctx, "causal", [P, P])
            c_c = count("causal_in")
            c_here = Q.dma(c_c, causal[:], a["k_causal"])
            NB = 4
            prob = [sb(tctx, "prob", [P, L]) for _ in range(NB)]
            probT = [sb(tctx, "probT", [P, SJ, P]) for _ in range(NB)]
            stat = [sb(tctx, "stat", [P, 8]) for _ in range(NB)]
            units = [(h, i) for h in range(NH) for i in range(SJ)]
            exp_done, prob_ready, probT_ready = {}, {}, {}
            prob_read, probT_read = [None] * NB, [None] * NB

            s_banks, t_banks, v_banks = (Ring(banks.tiles[i0:i1]) for i0, i1 in ((0, 4), (4, 6), (6, 8)))

            def softmax(n):
                h, i = units[n]
                b = n % NB
                keys = (i + 1) * P
                st = stat[b]
                pieces = [(k0, min(HALF, keys - k0)) for k0 in range(0, keys, HALF)]
                taken = []
                for k0, w in pieces:
                    nb, ps, free = s_banks.take()
                    m = mm(ps[:, 0:w], qT[0:QH, h, i * P:(i + 1) * P], kT[0:QH, h, k0:k0 + w], True, True, free)
                    taken.append((nb, ps, m))
                d0 = i * P - pieces[-1][0]
                ps = taken[-1][1]
                m_mask = tt(V, ps[:, d0:d0 + P], ps[:, d0:d0 + P], causal[:], ALU.add, taken[-1][2], c_here,
                            prob_ready.get(n - NB))
                for q, ((k0, w), (nb, ps, m)) in enumerate(zip(pieces, taken)):
                    V.do(lambda e, q=q, w=w, ps=ps: e.tensor_reduce(st[:, q:q + 1], ps[:, 0:w], AX.X, ALU.max),
                         m, m_mask)
                if len(pieces) == 2:
                    tt(V, st[:, 0:1], st[:, 0:1], st[:, 1:2], ALU.max)
                m_max = ts(V, st[:, 2:3], st[:, 0:1], -scale_qk, None, ALU.mult, None)
                for q, ((k0, w), (nb, ps, m)) in enumerate(zip(pieces, taken)):
                    m_e = act(prob[b][:, k0:k0 + w], ps[:, 0:w], ACT.Exp, m_max, prob_read[b],
                              bias=st[:, 2:3], scale=scale_qk, accum_out=st[:, 3 + q:4 + q])
                    s_banks.release(nb, m_e)
                exp_done[n] = m_e

            def normalise(n):
                h, i = units[n]
                b, keys = n % NB, (i + 1) * P
                st, m_e = stat[b], exp_done[n]
                if keys > HALF:
                    tt(V, st[:, 3:4], st[:, 3:4], st[:, 4:5], ALU.add, m_e)
                m_r = V.do(lambda e: e.reciprocal(st[:, 5:6], st[:, 3:4]), m_e)
                prob_ready[n] = ts(G, prob[b][:, 0:keys], prob[b][:, 0:keys], st[:, 5:6], None, ALU.mult, None, m_r)

            def turn_prob(n):
                h, i = units[n]
                b = n % NB
                for k0 in range(0, i + 1, 4):
                    kn = min(4, i + 1 - k0)
                    nb, ps, free = t_banks.take()
                    for k in range(kn):
                        m = transpose(ps[:, k * P:(k + 1) * P], prob[b][:, (k0 + k) * P:(k0 + k + 1) * P],
                                      prob_ready[n], free)
                    prob_read[b] = m
                    m = copy(S if k0 else V, probT[b][:, k0:k0 + kn, :],
                             ps[:, 0:kn * P].rearrange("p (k q) -> p k q", k=kn), m, probT_read[b])
                    t_banks.release(nb, m)
                    probT_ready.setdefault(n, []).append(m)

            def weigh_v(n):
                h, i = units[n]
                b, rows_ = n % NB, slice(h % 2 * 64, h % 2 * 64 + 64)
                nb, ps, free = v_banks.take()
                for k in range(i + 1):
                    m = mm(ps[rows_, 0:P], v_tok[:, k, h * VD:(h + 1) * VD], probT[b][:, k, :], k == 0, k == i,
                           probT_ready[n], free)
                probT_read[b] = m
                out_ = (rows_, h // 2, slice(i * P, (i + 1) * P))
                m1 = act(f_hi[out_], ps[rows_, 0:P], ACT.Copy, m)
                m2 = tt(V, f_lo[out_], ps[rows_, 0:P], f_hi[out_], ALU.subtract, m1)
                v_banks.release(nb, m1, m2)
                o_ready[h // 2] = [m1, m2]

            TURN, WEIGH = 3, 4
            for n in range(len(units) + WEIGH):
                if n < len(units):
                    softmax(n)
                if 1 <= n <= len(units):
                    normalise(n - 1)
                if 0 <= n - TURN < len(units):
                    turn_prob(n - TURN)
                if n >= WEIGH:
                    weigh_v(n - WEIGH)
        fence()

    op_hi = sb(run3, "op_hi", [P, KD, L], F32R, "right")
    op_lo = sb(run3, "op_lo", [P, KD, L], F32R, "right")
    op = (op_hi, op_lo)
    gin = Ring([sb(fctx, "ga_in", [P, 2, HALF]) for _ in range(2)], [count(f"ga_in{i}") for i in range(2)])
    nm = new_norm(fctx)
    x_here = Q.dma(count("x_back"), hT[:], x_dram.rearrange("(k p) t -> p k t", p=P))
    mix_ready = {}

    def to_mix(i, half, ps, m):
        s_, g, free = gin.take()
        Q.dma(gin.counts[s_], g[:, 0, :], z_tile(Z_GATE + i * P, half), free)
        here = Q.dma(gin.counts[s_], g[:, 1, :], mixb_dram[i * P:(i + 1) * P, hs(half)])
        m = tt(V, g[:, 0, :], ps[:], g[:, 0, :], ALU.mult, m, here)
        m1 = tt(V, g[:, 0, :], g[:, 0, :], g[:, 1, :], ALU.add)
        m2 = act(op_hi[:, i, hs(half)], g[:, 0, :], ACT.Copy, m1)
        m3 = tt(G, op_lo[:, i, hs(half)], g[:, 0, :], op_hi[:, i, hs(half)], ALU.subtract, m2)
        gin.release(s_, m2, m3)
        mix_ready.setdefault(i, []).extend([m2, m3])
        return [m]

    for b in range(2):
        f_read = linear(weights, (f_hi, f_lo), 4, [(i * P, 4 * b + i) for i in range(4)], to_mix, o_ready)

    for b in range(4):
        w_read = linear(weights, op, KD, [(0, 2 * b), (P, 2 * b + 1)],
                        residual_of(hT, lambda i, m: nm.add(hT[:, i, :], m), [x_here]), mix_ready)
    op_ready = split_scaled(hT, vec["g_ffn_2"], op_hi, op_lo, w_read)
    rs_ready = nm.finish(rs, D)
    f_tmp, f_free = gin.tiles[0], [gin.free[0]] * 2
    f_ready, next_ready = {}, {}
    V.wait(rs_ready)

    def to_squared(i, half, ps, m):
        t = f_tmp[:, half, :]
        m = tt(V, t, ps[:], rs[:, hs(half)], ALU.mult, m, f_free[half])
        m1 = stt(t, t, 0.0, t, ALU.max, ALU.mult)
        f_free[half] = list(split_to(f_hi, f_lo, t, i, half, m1, f_read))
        f_ready.setdefault(i, []).extend(f_free[half])
        return [m]

    def gate_operand(i, m):
        next_ready[i] = split_tile(i, hT[:, i, :], vec["g_ple_2"][:, i:i + 1], op_hi, op_lo, m, up_read)
        nm.add(hT[:, i, :], m)

    chunks = ffn_chunks(DFF2)
    for t0, nt in chunks:
        f_ready = {}
        for q in range(0, nt, 2):
            up_read = linear(weights, op, KD, [(0, q), (P, q + 1)], to_squared, op_ready)
        f_read = down(weights, (f_hi, f_lo), nt, f_ready,
                      residual_of(hT, gate_operand if t0 == chunks[-1][0] else None))

    V.wait(nm.finish(rs, D))
    used = now()
    for s_ in (V, S, G, Q):
        s_.wait(used)
    fctx.close()
    nm = new_norm(run3)
    proj = Ring([sb(run3, "proj", [P, HALF]) for _ in range(4)], [count(f"proj_in{i}") for i in range(4)])
    tmps = Ring([sb(run3, "ple_tmp", [P, HALF]) for _ in range(4)])
    scaled = {}

    def to_ple(i, half, ps, m):
        s_, tmp, free = tmps.take()
        t = tmp[:]
        p_, pr, p_free = proj.take()
        here = Q.dma(proj.counts[p_], pr[:], proj_dram[i * P:(i + 1) * P, hs(half)], p_free)
        m = tt(V, t, ps[:], rs[:, hs(half)], ALU.mult, m, free)
        m1 = act(t, t, ACT.Sigmoid, m)
        m2 = tt(G, t, t, pr[:], ALU.mult, m1, here)
        proj.release(p_, m2)
        m3 = tt(V, hT[:, i, hs(half)], hT[:, i, hs(half)], t, ALU.add, m2, next_ready[i])
        tmps.release(s_, m3)
        if half == 1:
            nm.add(hT[:, i, :], m3)
            scaled[i] = ts(V, hT[:, i, :], hT[:, i, :], vec["g_final_2"][:, i:i + 1], None, ALU.mult, None,
                           (S.done, S.done.value))
        return [m]

    for b in range(4):
        linear(weights, op, KD, [(0, 2 * b), (P, 2 * b + 1)], to_ple, next_ready)

    col_ = ncol[:, 0, :]
    m = nm.columns(col_)
    m = act(col_, col_, ACT.Sqrt, m, bias=eps_col, scale=1.0 / D)
    m_col = V.do(lambda e: e.reciprocal(col_, col_), m)
    out_view = out[0].rearrange("(t p) d -> t p d", p=P)
    rows_out = [sb(run3, "rows_out", [P, D])[:] for _ in range(4)]
    c_out = [count(f"out{i}") for i in range(4)]
    sent = [None] * 4
    for t in range(SJ):
        b = t % 4
        parts = []
        for q in range(2):
            n, ps, free = banks.take()
            for i in range(4):
                m = transpose(ps[:, i * P:(i + 1) * P], hT[:, q * 4 + i, t * P:(t + 1) * P],
                              scaled[q * 4 + i], free)
            o = rows_out[b][:, q * HALF:(q + 1) * HALF]
            if q:
                m = act(o, ps[:], ACT.Copy, m, m_col, sent[b], scale=col_[:, t:t + 1])
            else:
                m = ts(V, o, ps[:], col_[:, t:t + 1], None, ALU.mult, None, m, m_col, sent[b])
            banks.release(n, m)
            parts.append(m)
        sent[b] = Q.dma(c_out[b], out_view[t], rows_out[b], parts)
    run3.close()
    finish()
    main.close()




def constants():
    p = np.arange(P)
    f = np.float32
    vec_ = np.zeros((P, 16), f)
    vec_[:, 0] = EPS
    vec_[:, 1] = GN_EPS
    vec_[:, 2] = np.where(p < 64, 1, -1)
    vec_[:, 3] = np.where(p < 64, -1, 1)
    vec_[:, 4] = -1
    half = QR // 2
    vec_[:, 5] = (f(10000.0) ** (-np.arange(half, dtype=f) / f(half)))[p % half]
    vec_[:, 6] = np.where(p % QR < half, -1, 1)
    s, t = p[:, None] % C, np.arange(C)[None, :]
    key = np.arange(P)
    pool = np.stack([1.0 / np.minimum(np.arange(1, 17), w) for w in WINDOWS])
    return {
        "k_ident": np.eye(P, dtype=f),
        "k_ones": np.ones((P, P), f),
        "k_headones": (p[:, None] // 64 == p[None, :] // 64).astype(f),
        "k_swap": np.roll(np.eye(P, dtype=f), 64, axis=0),
        "k_vec": vec_,
        "k_wkv_mask": np.stack([t > s, t >= s], 1).astype(f).reshape(P, 2 * C),
        "k_chunk_mask": np.tile((np.arange(L) % C != 0).astype(f), (P, 1)),
        "k_causal": np.where(key[None, :] <= p[:, None], 0, -1e30).astype(f),
        "k_pool": np.tile(pool.astype(f).reshape(1, -1), (P, 1)),
    }


def kernel(**inputs):
    import concourse.bacc as bacc
    from concourse.bass_utils import run_bass_kernel_spmd

    nc = bacc.Bacc("TRN2", target_bir_lowering=False, num_devices=1)
    arrays = {n: np.ascontiguousarray(v) for n, v in inputs.items()} | constants()
    aps = {n: nc.dram_tensor("in_" + n, v.shape, mybir.dt.from_np(v.dtype), kind="ExternalInput").ap()
           for n, v in arrays.items()}
    out = nc.dram_tensor("out", (1, L, D), F32, kind="ExternalOutput").ap()
    build(nc, aps, out)
    result = run_bass_kernel_spmd(nc, [{"in_" + n: v for n, v in arrays.items()}], core_ids=[0])
    return result.results[0]["out"]
```
